# Optimizing a Trainium2 kernel written in Bass

```python
import jax, jax.numpy as jnp
from jax import lax
import numpy as np

D_MODEL = 1024
BATCH = 1
SEQ = 256
DEPTH = 2

D_MIX = D_MODEL
GMLP_HEADS = 8
FNET_GROUPS = 8
GMLP_WIDTH = D_MIX // 2
FNET_WIDTH = D_MIX - GMLP_WIDTH
GMLP_HEAD_DIM = GMLP_WIDTH // GMLP_HEADS
FNET_GROUP_DIM = FNET_WIDTH // FNET_GROUPS
CHUNK = 128
IN_COLS = 2 * GMLP_WIDTH + FNET_WIDTH
PEER_HEADS = 8
PEER_KEYS = 128
PEER_EXPERTS = PEER_KEYS * PEER_KEYS
PEER_TOPK = 16
PEER_QDIM = 256
PEER_HALF = PEER_QDIM // 2
PEER_BLOCK = 128
N_MOD = 6
EPS = 1e-6

kernel_name = 'hybrid_gmlp_fnet_peer_adaln'

def rms_norm(x, g):
    xf = x.astype(jnp.float32)
    y = xf * lax.rsqrt(jnp.mean(xf * xf, axis=-1, keepdims=True) + EPS)
    return (y * g.astype(jnp.float32)).astype(x.dtype)

def layer_norm_noaffine(x):
    xf = x.astype(jnp.float32)
    mu = jnp.mean(xf, axis=-1, keepdims=True)
    var = jnp.mean(jnp.square(xf - mu), axis=-1, keepdims=True)
    return ((xf - mu) * lax.rsqrt(var + EPS)).astype(x.dtype)

def modulate(h, shift, scale):
    return h * (1 + scale[:, None, :]) + shift[:, None, :]

def hybrid_mixer(h, w_in, ws, bs, fw, fb, gain_a, gain_b, w_out):
    B, S, _ = h.shape
    z = h @ w_in
    zu = z[..., :GMLP_WIDTH]
    zv = z[..., GMLP_WIDTH:2 * GMLP_WIDTH]
    zf = z[..., 2 * GMLP_WIDTH:]
    u = jax.nn.gelu(zu, approximate=False).reshape(B, S, GMLP_HEADS, GMLP_HEAD_DIM)
    v = layer_norm_noaffine(jax.nn.gelu(zv, approximate=False).reshape(B, S, GMLP_HEADS, GMLP_HEAD_DIM))
    v = v.reshape(B, S // CHUNK, CHUNK, GMLP_HEADS, GMLP_HEAD_DIM)
    sv = jnp.einsum('hpq,bcqhd->bcphd', ws, v) + bs.T[None, None, :, :, None]
    y_a = (u * sv.reshape(B, S, GMLP_HEADS, GMLP_HEAD_DIM)).reshape(B, S, GMLP_WIDTH)
    f = zf.reshape(B, S, FNET_GROUPS, FNET_GROUP_DIM).astype(jnp.float32)
    fr = jnp.fft.fft2(f, axes=(1, 3), norm='ortho').real.astype(h.dtype)
    y_b = (jnp.einsum('bsgd,gde->bsge', fr, fw) + fb[None, None]).reshape(B, S, FNET_WIDTH)
    y = jnp.concatenate([rms_norm(y_a, gain_a), rms_norm(y_b, gain_b)], axis=-1)
    return y @ w_out

def peer_ffn(h, wq, k1, k2, U, V):
    B, S, D = h.shape
    hb = h.reshape(B * S // PEER_BLOCK, PEER_BLOCK, D)

    def block(hc):
        q = (hc @ wq).reshape(PEER_BLOCK, PEER_HEADS, 2, PEER_HALF)
        s1 = jnp.einsum('thd,hnd->thn', q[:, :, 0], k1).astype(jnp.float32)
        s2 = jnp.einsum('thd,hnd->thn', q[:, :, 1], k2).astype(jnp.float32)
        v1, i1 = lax.top_k(s1, PEER_TOPK)
        v2, i2 = lax.top_k(s2, PEER_TOPK)
        cand = (v1[..., :, None] + v2[..., None, :]).reshape(PEER_BLOCK, PEER_HEADS, PEER_TOPK * PEER_TOPK)
        cidx = (i1[..., :, None] * PEER_KEYS + i2[..., None, :]).reshape(PEER_BLOCK, PEER_HEADS, PEER_TOPK * PEER_TOPK)
        sc, pos = lax.top_k(cand, PEER_TOPK)
        eidx = jnp.take_along_axis(cidx, pos, axis=-1).reshape(PEER_BLOCK, PEER_HEADS * PEER_TOPK)
        g = jax.nn.softmax(sc, axis=-1).reshape(PEER_BLOCK, PEER_HEADS * PEER_TOPK).astype(hc.dtype)
        u_sel = jnp.take(U, eidx, axis=0)
        a = jax.nn.gelu(jnp.einsum('td,tkd->tk', hc, u_sel), approximate=False)
        v_sel = jnp.take(V, eidx, axis=0)
        return jnp.einsum('tk,tkd->td', g * a, v_sel)

    return lax.map(block, hb).reshape(B, S, D)

def setup_inputs(seed: int = 0) -> dict:
    key = jax.random.key(seed)
    ks = jax.random.split(key, 22)

    def nrm(k, shape, scale):
        return jax.random.normal(k, shape, jnp.float32) * scale

    L, D = DEPTH, D_MODEL
    return {
        'x': nrm(ks[0], (BATCH, SEQ, D), 1.0),
        'c': nrm(ks[1], (BATCH, D), 1.0),
        'mod_w': nrm(ks[2], (L, D, N_MOD * D), D ** -0.5),
        'mod_b': nrm(ks[3], (L, N_MOD * D), 0.02),
        'norm1_g': 1.0 + nrm(ks[4], (L, D), 0.02),
        'w_in': nrm(ks[5], (L, D, IN_COLS), D ** -0.5),
        'gmlp_ws': nrm(ks[6], (L, GMLP_HEADS, CHUNK, CHUNK), CHUNK ** -0.5),
        'gmlp_bs': 1.0 + nrm(ks[7], (L, GMLP_HEADS, CHUNK), 0.02),
        'fnet_w': nrm(ks[8], (L, FNET_GROUPS, FNET_GROUP_DIM, FNET_GROUP_DIM), FNET_GROUP_DIM ** -0.5),
        'fnet_b': nrm(ks[9], (L, FNET_GROUPS, FNET_GROUP_DIM), 0.02),
        'gain_a': 1.0 + nrm(ks[10], (L, GMLP_WIDTH), 0.02),
        'gain_b': 1.0 + nrm(ks[11], (L, FNET_WIDTH), 0.02),
        'w_out': nrm(ks[12], (L, D_MIX, D), D_MIX ** -0.5),
        'norm2_g': 1.0 + nrm(ks[13], (L, D), 0.02),
        'peer_wq': nrm(ks[14], (L, D, PEER_HEADS * PEER_QDIM), D ** -0.5),
        'peer_k1': nrm(ks[15], (L, PEER_HEADS, PEER_KEYS, PEER_HALF), PEER_HALF ** -0.5),
        'peer_k2': nrm(ks[16], (L, PEER_HEADS, PEER_KEYS, PEER_HALF), PEER_HALF ** -0.5),
        'peer_u': nrm(ks[17], (L, PEER_EXPERTS, D), D ** -0.5),
        'peer_v': nrm(ks[18], (L, PEER_EXPERTS, D), PEER_HEADS ** -0.5),
        'final_g': 1.0 + nrm(ks[19], (D,), 0.02),
    }

def reference(x, c, mod_w, mod_b, norm1_g, w_in, gmlp_ws, gmlp_bs, fnet_w, fnet_b,
              gain_a, gain_b, w_out, norm2_g, peer_wq, peer_k1, peer_k2, peer_u, peer_v, final_g):
    sc_in = jax.nn.silu(c)
    for l in range(DEPTH):
        mod = sc_in @ mod_w[l] + mod_b[l]
        sh1, scl1, g1, sh2, scl2, g2 = jnp.split(mod, N_MOD, axis=-1)
        h = modulate(rms_norm(x, norm1_g[l]), sh1, scl1)
        x = x + g1[:, None, :] * hybrid_mixer(h, w_in[l], gmlp_ws[l], gmlp_bs[l], fnet_w[l], fnet_b[l],
                                              gain_a[l], gain_b[l], w_out[l])
        h = modulate(rms_norm(x, norm2_g[l]), sh2, scl2)
        x = x + g2[:, None, :] * peer_ffn(h, peer_wq[l], peer_k1[l], peer_k2[l], peer_u[l], peer_v[l])
    return rms_norm(x, final_g)


_drawn_inputs = setup_inputs


def setup_inputs(seed=0):
    import zlib

    import numpy as np

    out = dict(_drawn_inputs(seed))
    spreads = {}
    factors = {'gmlp_bs': 12.944,
     'gain_a': 10.27,
     'gain_b': 9.858,
     'final_g': 22.987,
     'fnet_b': 2.849,
     'norm2_g': 13.752}
    for name, (base, spread) in spreads.items():
        noise = np.random.default_rng([zlib.crc32(name.encode()), seed]).standard_normal(out[name].shape)
        drawn = base * np.exp(spread * noise) if base else spread * noise
        out[name] = __import__('jax').numpy.asarray(drawn.astype(out[name].dtype))
    for name, factor in factors.items():
        out[name] = (out[name] * factor).astype(out[name].dtype)
    return out
```

```python
from contextlib import ExitStack

import numpy as np

import concourse.bass as bass
from concourse import mybir

F32 = mybir.dt.float32
U32 = mybir.dt.uint32
BF16 = mybir.dt.bfloat16
ALU = mybir.AluOpType
ACT = mybir.ActivationFunctionType
AX = mybir.AxisListType

P = 128
D = 1024
T = 256
LAYERS = 2
KC = D // P
TB = T // P
HEADS = 8
HD = 64
HALF = HEADS * HD
IN_COLS = 3 * HALF
CB = D // P
PAIRS = HALF // P
EPS = 1e-6
KEYS = 128
TOPK = 16
ROWS = 2 * HEADS
QCOLS = ROWS * P
CHUNKS = KEYS
N_MOD = 6
MODS = N_MOD * KC
NEG = -3.0e38

SLOTS = 8
PER_DMA = 2
QUEUES = SLOTS // PER_DMA
MOD_ROUNDS = MODS // SLOTS
EXP_ROUNDS = CHUNKS // SLOTS
ROUNDS = MOD_ROUNDS + 2 * EXP_ROUNDS
TILES = ROUNDS * SLOTS
EARLY_ROUNDS = EXP_ROUNDS // 2

GT = 8
OT = 4
GROUPS = T // GT
PBANKS = 4

C_ID, C_IOTA, C_ONES, C_COSD, C_SIND = (i * P for i in range(5))
C_COSS = 5 * P
C_SINS = C_COSS + TB * T
N_CONST = C_SINS + TB * T
S_NORM1, S_NORM2, S_GAIN, S_BS, S_MODB = 0, 8, 16, 24, 32
S_FW = S_MODB + MODS
S_WS = S_FW + PAIRS * HD
N_SMALL = S_WS + HEADS * P


def build(nc, x_in, c_in, consts_in, small_in, fb_in, keys_in, w_in_in, w_out_in, wq_in, mod_in, u_in, v_in,
          final_in, out):
    ctx = ExitStack()
    with ctx:
        def sb(name, shape, dt=F32):
            return ctx.enter_context(nc.sbuf_tensor(name, shape, dt))

        def sem(name):
            return ctx.enter_context(nc.semaphore(name))

        big = sb("expert_acts", [P, CHUNKS * T])
        xT = sb("xT", [P, KC, T])
        hT = sb("hT", [P, KC, T])
        ring = sb("ring", [P, SLOTS, D])
        keys = sb("keys", [P, ROWS, KEYS])
        small = sb("small", [P, N_SMALL])
        consts = sb("consts", [P, N_CONST])
        kT = sb("routed", [P, 3, T])
        picks = sb("picks", [P, TB, 3, P])
        modT = sb("modT", [P, MODS])
        ab = sb("ab", [P, 2, KC])
        cT = sb("cT", [P, KC])
        siluT = sb("siluT", [P, KC])
        final_g = sb("final_g", [P, KC])
        rstd = sb("rstd", [P, 2, T])
        stat = sb("stat", [P, 4, ROWS])
        mstat = sb("mstat", [P, 3, 4])
        zeros = sb("zeros", [P, 640], BF16)

        w_in_sb = big[:, 0:KC * IN_COLS].rearrange("p (k n) -> p k n", k=KC)
        FB_AT = KC * IN_COLS
        fblock = big[:, FB_AT:FB_AT + PAIRS * 256].rearrange("p (r s g e) -> p r s g e", r=PAIRS, s=2, g=2)
        fb_row = big[:, FB_AT + 1024:FB_AT + 1024 + HALF]
        wq_sb = big[:, 0:KC * QCOLS].rearrange("p (k n) -> p k n", k=KC)
        M0 = KC * QCOLS
        uv = big[:, M0:M0 + 2048].rearrange("p (b s n) -> p b s n", b=TB, s=2)
        zfT = big[:, M0 + 2048:M0 + 3072].rearrange("p (r t) -> p r t", r=PAIRS)
        rt = big[:, M0 + 3072:M0 + 5120].rearrange("p (b s n) -> p b s n", b=TB, s=2)
        yb = big[:, M0 + 5120:M0 + 6144].rearrange("p (b n) -> p b n", b=TB)
        yT = big[:, M0 + 6144:M0 + 8192].rearrange("p (c t) -> p c t", c=CB)
        sqv = yT
        qT = big[:, M0:M0 + 4096].rearrange("p (r t) -> p r t", r=ROWS)
        scores = big[:, M0 + 4096:M0 + 8192].rearrange("p (b r n) -> p b r n", b=TB, r=ROWS)
        w_out_sb = big[:, M0 + 8192:M0 + 16384].rearrange("p (c n) -> p c n", c=CB)
        R0 = M0 + 8192
        left = big[:, R0:R0 + 2048]
        cand = big[:, R0 + 2048:R0 + 4096]
        eq = big[:, R0 + 4096:R0 + 6144]
        at = [R0 + 6144]

        def scratch(n, dt=F32):
            a = big[:, at[0]:at[0] + n]
            at[0] += n
            return a if dt == F32 else a.bitcast(dt)

        top_v = scratch(ROWS * TOPK).rearrange("p (r k) -> p r k", r=ROWS)
        top_iu = scratch(ROWS * TOPK, U32).rearrange("p (r k) -> p r k", r=ROWS)
        top_i = scratch(ROWS * TOPK).rearrange("p (h s k) -> p h s k", h=HEADS, s=2)
        pick_v = scratch(P).rearrange("p (h k) -> p h k", h=HEADS)
        pick_u = scratch(P, U32)
        half_u = scratch(2 * P, U32).rearrange("p (s n) -> p s n", s=2)
        half_f = scratch(2 * P).rearrange("p (s n) -> p s n", s=2)
        gsum = scratch(2 * HEADS).rearrange("p (s h) -> p s h", s=2)
        assert at[0] <= CHUNKS * T

        hot1 = keys[:, 0:8, :]
        hot2 = keys[:, 8:16, :]

        ident = consts[:, C_ID:C_ID + P]
        iota = consts[:, C_IOTA:C_IOTA + P]
        ones = consts[:, C_ONES:C_ONES + P]

        ps = ctx.enter_context(nc.psum_tensor("ps", [P, 8, 512], F32))
        ps_v = ps[:, 0:4, :].rearrange("p b (h t) -> p (b h) t", h=2)
        ps_o = ps[:, 4:8, :].rearrange("p b (h t) -> p (b h) t", h=2)

        once = sem("once_loaded")
        small_ld, keys_ld, fb_ld = sem("small_loaded"), sem("keys_loaded"), sem("fb_loaded")
        win_ld, wout_ld, wq_ld = sem("w_in_loaded"), sem("w_out_loaded"), sem("wq_loaded")
        ring_full = [sem(f"ring_full{q}") for q in range(QUEUES)]
        tile_free = sem("tile_free")
        root_in, ms_in, fin_in = sem("root_in"), sem("ms_in"), sem("fin_in")
        silu_done = sem("silu_done")
        sq_done, sum_mm, root_done = sem("sq_done"), sem("sum_mm"), sem("root_done")
        h_done = sem("h_done")
        fw_mm, fw_done = sem("fw_mm"), sem("fw_done")
        z_mm, gelu_done, zf_done = sem("z_mm"), sem("gelu_done"), sem("zf_done")
        ln_var, ln_root, ln_done = sem("ln_var"), sem("ln_root"), sem("ln_done")
        sv_mm, ya_done = sem("sv_mm"), sem("ya_done")
        rt_mm, rt_done = sem("rt_mm"), sem("rt_done")
        y_mm, yb_done = sem("y_mm"), sem("yb_done")
        ms_done, ms_root, yn_done = sem("ms_done"), sem("ms_root"), sem("yn_done")
        tr_mm, yt_done = sem("tr_mm"), sem("yt_done")
        out_mm, x_done = sem("out_mm"), sem("x_done")
        q_mm, q_done = sem("q_mm"), sem("q_done")
        s_mm, s_done = sem("s_mm"), sem("s_done")
        exp_in, exp_done = sem("exp_in"), sem("exp_done")
        picks_done, kt_mm, kt_done = sem("picks_done"), sem("kt_mm"), sem("kt_done")
        p_free, p_done = sem("p_free"), sem("p_done")
        hot_ready, hot_free = sem("hot_ready"), sem("hot_free")
        g_free = sem("g_free")
        dve_step = sem("dve_step")
        zeros_done = sem("zeros_done")
        dve_held, pe_held = sem("dve_held"), sem("pe_held")
        fin_sq, fin_mm, fin_root, fin_done = sem("fin_sq"), sem("fin_mm"), sem("fin_root"), sem("fin_done")
        out_st = sem("out_stored")
        DVE_STEPS = 54

        block = ctx.enter_context(nc.Block())

        @block.sync
        def _(sp):
            def stream(l, first, rounds, src):
                with sp.Fori(0, rounds) as r:
                    for q in range(QUEUES):
                        sp.wait_ge(tile_free, (l * ROUNDS + first + r) * SLOTS + (q + 1) * PER_DMA)
                        sp.dma_start(ring[:, q * PER_DMA:(q + 1) * PER_DMA, :],
                                     src[bass.ds(l, 1), bass.ds(r * QUEUES + q, 1)].rearrange(
                                         "a b p (s n) -> (a b p) s n", s=PER_DMA)).then_inc(ring_full[q], 16)

            with sp.Fori(0, LAYERS) as l:
                stream(l, 0, MOD_ROUNDS, mod_in)
                stream(l, MOD_ROUNDS, EXP_ROUNDS, u_in)
                stream(l, MOD_ROUNDS + EXP_ROUNDS, EXP_ROUNDS, v_in)
            sp.wait_ge(fin_done, 1)
            sp.dma_start(out, hT[:]).then_inc(out_st, 16)
            sp.wait_ge(out_st, 16)

        @block.gpsimd
        def _(pool):
            pool.dma_start(cT[:], c_in).then_inc(once, 16)
            pool.dma_start(xT[:], x_in).then_inc(once, 16)
            pool.dma_start(consts[:], consts_in).then_inc(once, 16)
            pool.dma_start(final_g[:], final_in).then_inc(once, 16)
            with pool.Fori(0, LAYERS) as l:
                pool.wait_ge(x_done, 2 * l + 1)
                pool.dma_start(small[:], small_in[bass.ds(l, 1)].rearrange("a p n -> (a p) n")).then_inc(small_ld, 16)
                pool.dma_start(w_in_sb, w_in_in[bass.ds(l, 1)].rearrange("a p k n -> (a p) k n")).then_inc(win_ld, 16)
                pool.dma_start(fb_row, fb_in[bass.ds(l, 1)].to_broadcast([P, HALF])).then_inc(fb_ld, 16)
                pool.dma_start(w_out_sb, w_out_in[bass.ds(l, 1)].rearrange("a p k n -> (a p) k n")).then_inc(wout_ld, 16)
                pool.dma_start(keys[:], keys_in[bass.ds(l, 1)].rearrange("a p k n -> (a p) k n")).then_inc(keys_ld, 16)
                pool.wait_ge(z_mm, 8 * l + 8)
                pool.wait_ge(rt_mm, 2 * l + 2)
                pool.wait_ge(yb_done, 2 * l + 2)
                pool.dma_start(wq_sb, wq_in[bass.ds(l, 1)].rearrange("a p k n -> (a p) k n")).then_inc(wq_ld, 16)

        @block.tensor
        def _(pe):
            def mm(out, lhsT, rhs, start, stop):
                return nc.tensor.matmul(out, lhsT, rhs, start=start, stop=stop, skip_group_check=True)

            def column_sums(bank):
                for k in range(KC):
                    m = mm(ps[:, bank, 0:T], ones, hT[:, k, :], k == 0, k == KC - 1)
                return m

            pe.sem_inc(tile_free, SLOTS)
            pe.wait_ge(once, 64)
            pe.wait_ge(silu_done, 1)
            pe.wait_ge(zeros_done, 1)
            with pe.Fori(0, LAYERS) as l:
                with pe.Fori(0, MOD_ROUNDS) as r:
                    for s in range(SLOTS):
                        if s % PER_DMA == 0:
                            pe.wait_ge(ring_full[s // PER_DMA], 16 * (l * ROUNDS + r + 1))
                        for k in range(KC):
                            m = mm(ps[:, 7, bass.ds(r * SLOTS + s, 1)], ring[:, s, k * P:(k + 1) * P],
                                   siluT[:, k:k + 1], k == 0, k == KC - 1)
                        m.then_inc(tile_free, 1)
                pe.wait_ge(small_ld, 16 * l + 16)
                mm(ps[:, 5, 0:256], consts[:, C_COSD:C_COSD + P], small[:, S_FW:S_FW + 256], True, True)
                mm(ps[:, 5, 256:512], consts[:, C_SIND:C_SIND + P], small[:, S_FW:S_FW + 256], True, True)\
                    .then_inc(fw_mm, 1)
                pe.wait_ge(sq_done, 2 * l + 1)
                column_sums(6).then_inc(sum_mm, 1)
                pe.wait_ge(h_done, 2 * l + 1)
                pe.wait_ge(win_ld, 16 * l + 16)
                for s in range(2):
                    for b in range(TB):
                        for k in range(KC):
                            m = mm(ps[:, 2 * b + (1 - s), :], hT[:, k, b * P:(b + 1) * P],
                                   w_in_sb[:, k, (1 - s) * HALF:(2 - s) * HALF], k == 0, k == KC - 1)
                        m.then_inc(z_mm, 1)
                pe.wait_ge(fw_done, l + 1)
                for r in range(PAIRS):
                    for k in range(KC):
                        m = mm(ps[:, 4 + r // 2, (r % 2) * T:(r % 2 + 1) * T],
                               w_in_sb[:, k, 2 * HALF + r * P:2 * HALF + (r + 1) * P], hT[:, k, :],
                               k == 0, k == KC - 1)
                    m.then_inc(z_mm, 1)
                pe.wait_ge(ln_done, l + 1)
                for h in range(HEADS):
                    m = mm(ps[:, 6 + h // 4, (h % 4) * P:(h % 4 + 1) * P], small[:, S_WS + h * P:S_WS + (h + 1) * P],
                           uv[:, :, 1, h * HD:(h + 1) * HD], True, True)
                m.then_inc(sv_mm, 1)
                pe.wait_ge(zf_done, 2 * l + 2)
                pe.wait_ge(gelu_done, 4 * l + 4)
                for b in range(TB):
                    for r in range(PAIRS):
                        m = mm(ps[:, 2 * b + r // 2, (r % 2) * 256:(r % 2 + 1) * 256], zfT[:, r, b * P:(b + 1) * P],
                               fblock[:, r].rearrange("p s g e -> p (s g e)"), True, True)
                    m.then_inc(rt_mm, 1)
                pe.wait_ge(rt_done, 2 * l + 2)
                for tp in range(TB):
                    n = 0
                    for b in range(TB):
                        for s, at_ in enumerate((C_COSS, C_SINS)):
                            m = mm(ps[:, 4 + tp, :], consts[:, at_ + b * T + tp * P:at_ + b * T + (tp + 1) * P],
                                   rt[:, b, s, :], n == 0, n == 2 * TB - 1)
                            n += 1
                    m.then_inc(y_mm, 1)
                pe.wait_ge(yn_done, l + 1)
                for g in range(2):
                    for c in range(CB // 2):
                        for b in range(TB):
                            src = uv[:, b, 0, c * P:(c + 1) * P] if g == 0 else yb[:, b, c * P:(c + 1) * P]
                            m = nc.tensor.transpose(ps[:, 2 * g + c // 2, (c % 2) * T + b * P:(c % 2) * T + (b + 1) * P],
                                                    src, ident)
                    m.then_inc(tr_mm, 1)
                pe.wait_ge(yt_done, l + 1)
                pe.wait_ge(wout_ld, 16 * l + 16)
                for d in range(KC):
                    for c in range(CB):
                        m = mm(ps_o[:, d, :], w_out_sb[:, c, d * P:(d + 1) * P], yT[:, c, :], c == 0, c == CB - 1)
                m.then_inc(out_mm, 1)
                pe.wait_ge(sq_done, 2 * l + 2)
                column_sums(0).then_inc(sum_mm, 1)
                pe.wait_ge(h_done, 2 * l + 2)
                pe.wait_ge(wq_ld, 16 * l + 16)
                for r in range(ROWS):
                    for k in range(KC):
                        m = mm(ps[:, r // 2, (r % 2) * T:(r % 2 + 1) * T], wq_sb[:, k, r * P:(r + 1) * P], hT[:, k, :],
                               k == 0, k == KC - 1)
                    if r % 2:
                        m.then_inc(q_mm, 1)
                pe.wait_ge(keys_ld, 16 * l + 16)
                for b in range(TB):
                    pe.wait_ge(q_done, 8 * l + 8)
                    for r in range(ROWS):
                        m = mm(ps[:, 4 - 4 * b + r // 4, (r % 4) * P:(r % 4 + 1) * P], qT[:, r, b * P:(b + 1) * P],
                               keys[:, r, :], True, True)
                    m.then_inc(s_mm, 1)

                def expert_in(first, rounds):
                    with pe.Fori(first, first + rounds) as r:
                        for s in range(SLOTS):
                            if s % PER_DMA == 0:
                                pe.wait_ge(ring_full[s // PER_DMA], 16 * (l * ROUNDS + MOD_ROUNDS + r + 1))
                            pe.wait_ge(p_free, l * (CHUNKS + PBANKS) + r * SLOTS + s + 1)
                            for k in range(KC):
                                m = mm(ps[:, s % PBANKS, 0:T], ring[:, s, k * P:(k + 1) * P], hT[:, k, :],
                                       k == 0, k == KC - 1)
                            m.then_inc(tile_free, 1)

                expert_in(0, EARLY_ROUNDS)
                for b in range(TB):
                    pe.wait_ge(picks_done, 2 * l + b + 1)
                    for i in range(3):
                        m = nc.tensor.transpose(ps[:, 4 + b, i * P:(i + 1) * P], picks[:, b, i, :], ident)
                    m.then_inc(kt_mm, 1)
                expert_in(EARLY_ROUNDS, EXP_ROUNDS - EARLY_ROUNDS)
                pe.wait_ge(kt_done, 2 * l + 2)
                pe.sem_inc(pe_held, 1)
                with pe.Fori(0, GROUPS // 2) as i:
                    for g in range(2):
                        pe.wait_ge(g_free, l * (GROUPS + 2) + i * 2 + g + 1)
                        for o in range(GT // OT):
                            pe.wait_ge(hot_ready, l * (T // OT) + i * 4 + g * 2 + o + 1)
                            for t in range(OT):
                                j = o * OT + t
                                m = mm(ps[:, 4 + 2 * g + o, t * P:(t + 1) * P], hot1[:, j, :], hot2[:, j, :], True, True)
                            m.then_inc(hot_free, 1)
                pe.wait_ge(p_done, l + 1)
                pe.wait_ge(g_free, (l + 1) * (GROUPS + 2))
                for b in range(4):
                    mm(ps[:, b, :], zeros[:, 0:P], zeros[:, P:P + 512], True, False)
                with pe.Fori(0, EXP_ROUNDS) as r:
                    for s in range(SLOTS):
                        if s % PER_DMA == 0:
                            pe.wait_ge(ring_full[s // PER_DMA], 16 * (l * ROUNDS + MOD_ROUNDS + EXP_ROUNDS + r + 1))
                        for d in range(KC):
                            m = mm(ps_v[:, d, :], ring[:, s, d * P:(d + 1) * P],
                                   big[:, bass.ds(r * (SLOTS * T) + s * T, T)], False, False)
                        m.then_inc(tile_free, 1)
            pe.wait_ge(fin_sq, 1)
            column_sums(6).then_inc(fin_mm, 1)

        @block.scalar
        def _(act):
            act.wait_ge(once, 64)
            nc.scalar.activation(siluT[:], cT[:], ACT.Silu).then_inc(silu_done, 1)
            with act.Fori(0, LAYERS) as l:
                act.wait_ge(x_done, 2 * l + 1)
                nc.scalar.activation(hT[:], xT[:], ACT.Square).then_inc(sq_done, 1)
                act.wait_ge(root_in, 2 * l + 1)
                nc.scalar.activation(rstd[:, 1, :], rstd[:, 0, :], ACT.Sqrt).then_inc(root_done, 1)
                for s in range(2):
                    for b in range(TB):
                        act.wait_ge(z_mm, 8 * l + 2 * s + b + 1)
                        nc.scalar.activation(uv[:, b, 1 - s, :], ps[:, 2 * b + (1 - s), :], ACT.Gelu).then_inc(gelu_done, 1)
                act.wait_ge(ln_var, l + 1)
                nc.scalar.activation(stat[:, 3, :], stat[:, 2, :], ACT.Sqrt).then_inc(ln_root, 1)
                for b in range(TB):
                    act.wait_ge(rt_mm, 2 * l + b + 1)
                    src = ps[:, 2 * b:2 * b + 2, :].rearrange("p c (r s n) -> p (c r) s n", r=2, s=2)
                    nc.scalar.activation(rt[:, b].rearrange("p s (r n) -> p r s n", r=PAIRS), src, ACT.Copy)\
                        .then_inc(rt_done, 1)
                act.wait_ge(ya_done, l + 1)
                act.wait_ge(y_mm, 2 * l + 2)
                for b in range(TB):
                    nc.scalar.activation(rt[:, b, 0, :], uv[:, b, 0, :], ACT.Square, accum_out=mstat[:, 0, b:b + 1])
                act.wait_ge(yb_done, 2 * l + 2)
                for b in range(TB):
                    m = nc.scalar.activation(rt[:, b, 1, :], yb[:, b, :], ACT.Square, accum_out=mstat[:, 0, 2 + b:3 + b])
                m.then_inc(ms_done, 1)
                act.wait_ge(ms_in, l + 1)
                nc.scalar.activation(mstat[:, 2, :], mstat[:, 1, :], ACT.Sqrt).then_inc(ms_root, 1)
                act.wait_ge(x_done, 2 * l + 2)
                nc.scalar.activation(hT[:], xT[:], ACT.Square).then_inc(sq_done, 1)
                act.wait_ge(root_in, 2 * l + 2)
                nc.scalar.activation(rstd[:, 1, :], rstd[:, 0, :], ACT.Sqrt).then_inc(root_done, 1)
                for i in range(ROWS // 2):
                    act.wait_ge(q_mm, 8 * l + i + 1)
                    nc.scalar.activation(qT[:, 2 * i:2 * i + 2, :],
                                         ps[:, i, :].rearrange("p (r t) -> p r t", r=2), ACT.Copy).then_inc(q_done, 1)
                for b in range(TB):
                    act.wait_ge(s_mm, 2 * l + b + 1)
                    nc.scalar.activation(scores[:, b], ps[:, 4 - 4 * b:8 - 4 * b, :].rearrange(
                        "p c (r n) -> p (c r) n", r=4), ACT.Copy).then_inc(s_done, 1)
                act.wait_ge(s_done, 2 * l + 2)
                act.sem_inc(p_free, PBANKS)
                for b in range(TB):
                    act.wait_ge(exp_in, 2 * l + b + 1)
                    g = picks[:, b, 2, :]
                    nc.scalar.activation(g, g, ACT.Exp).then_inc(exp_done, 1)

                def gelus(first, rounds):
                    with act.Fori(first, first + rounds) as r:
                        for s in range(SLOTS):
                            act.wait_ge(tile_free, SLOTS + l * TILES + MODS + r * SLOTS + s + 1)
                            nc.scalar.activation(big[:, bass.ds(r * (SLOTS * T) + s * T, T)], ps[:, s % PBANKS, 0:T],
                                                 ACT.Gelu).then_inc(p_free, 1)

                gelus(0, EARLY_ROUNDS)
                act.wait_ge(kt_done, 2 * l + 2)
                gelus(EARLY_ROUNDS, EXP_ROUNDS - EARLY_ROUNDS)
                act.wait_ge(p_free, (l + 1) * (CHUNKS + PBANKS))
                act.sem_inc(p_done, 1)
            act.wait_ge(x_done, 2 * LAYERS + 1)
            nc.scalar.activation(hT[:], xT[:], ACT.Square).then_inc(fin_sq, 1)
            act.wait_ge(fin_in, 1)
            nc.scalar.activation(rstd[:, 1, :], rstd[:, 0, :], ACT.Sqrt).then_inc(fin_root, 1)

        @block.vector
        def _(dve):
            v = nc.vector
            v.memset(zeros[:], 0.0).then_inc(zeros_done, 1)
            dve.wait_ge(once, 64)
            dve.sem_inc(x_done, 1)

            def norm(l, n, bank):
                dve.wait_ge(sum_mm, 2 * l + n + 1)
                v.tensor_scalar(rstd[:, 0, :], ps[:, bank, 0:T], 1.0 / D, EPS, ALU.mult, ALU.add).then_inc(root_in, 1)
                dve.wait_ge(root_done, 2 * l + n + 1)
                step(v.reciprocal(rstd[:, 0, :], rstd[:, 1, :]))
                step(v.tensor_tensor(hT[:], xT[:], rstd[:, 0, :].unsqueeze(1).to_broadcast([P, KC, T]), ALU.mult))
                for k in range(KC):
                    m = v.tensor_scalar(hT[:, k, :], hT[:, k, :], ab[:, n, k:k + 1],
                                        modT[:, 3 * KC * n + k:3 * KC * n + k + 1], ALU.mult, ALU.add)
                m.then_inc(h_done, 1)

            with dve.Fori(0, LAYERS) as l:
                k_step = [0]

                def step(m, hold=False):
                    k_step[0] += 1
                    m.then_inc(dve_step, 1)
                    dve.wait_ge(dve_step, l * DVE_STEPS + k_step[0])
                    if hold:
                        dve.sem_inc(dve_held, 1)

                step(v.memset(fblock, 0.0))
                dve.wait_ge(small_ld, 16 * l + 16)
                dve.wait_ge(tile_free, SLOTS + l * TILES + MODS)
                step(v.tensor_tensor(modT[:], ps[:, 7, 0:MODS], small[:, S_MODB:S_MODB + MODS], ALU.add))
                for n, at_ in enumerate((S_NORM1, S_NORM2)):
                    m = v.scalar_tensor_tensor(out=ab[:, n, :], in0=modT[:, (3 * n + 1) * KC:(3 * n + 2) * KC], scalar=1.0,
                                               in1=small[:, at_:at_ + KC], op0=ALU.add, op1=ALU.mult)
                step(m)
                dve.wait_ge(fw_mm, l + 1)
                for g in range(2):
                    half = slice(g * HD, (g + 1) * HD)
                    for s in range(2):
                        m = v.tensor_copy(fblock[half, :, s, g, :],
                                          ps[half, 5, s * 256:(s + 1) * 256].rearrange("p (r e) -> p r e", r=PAIRS))
                m.then_inc(fw_done, 1)
                norm(l, 0, 6)
                dve.wait_ge(gelu_done, 4 * l + 2)
                vh = uv[:, :, 1, :].rearrange("p b (h d) -> p b h d", h=HEADS)
                sqh = sqv[:, 0:4, :].rearrange("p c t -> p (c t)").rearrange("p (b h d) -> p b h d", b=TB, h=HEADS)

                def st(i):
                    return stat[:, i, :].rearrange("p (b h) -> p b h", b=TB)

                def wide(i):
                    return st(i).unsqueeze(3).to_broadcast([P, TB, HEADS, HD])

                step(v.tensor_reduce(st(0), vh, AX.X, ALU.add))
                step(v.tensor_scalar(stat[:, 1, :], stat[:, 0, :], -1.0 / HD, None, ALU.mult))
                step(v.tensor_tensor(vh, vh, wide(1), ALU.add))
                step(v.tensor_tensor(sqh, vh, vh, ALU.mult))
                step(v.tensor_reduce(st(0), sqh, AX.X, ALU.add))
                v.tensor_scalar(stat[:, 2, :], stat[:, 0, :], 1.0 / HD, EPS, ALU.mult, ALU.add).then_inc(ln_var, 1)
                dve.wait_ge(ln_root, l + 1)
                step(v.reciprocal(stat[:, 1, :], stat[:, 3, :]))
                v.tensor_tensor(vh, vh, wide(1), ALU.mult).then_inc(ln_done, 1)
                for i in range(2):
                    dve.wait_ge(z_mm, 8 * l + 6 + 2 * i)
                    v.tensor_copy(zfT[:, 2 * i:2 * i + 2, :], ps[:, 4 + i, :].rearrange("p (r t) -> p r t", r=2))\
                        .then_inc(zf_done, 1)
                dve.wait_ge(sv_mm, l + 1)
                dve.wait_ge(gelu_done, 4 * l + 4)
                for h in range(HEADS):
                    u = uv[:, :, 0, h * HD:(h + 1) * HD]
                    m = v.scalar_tensor_tensor(out=u, in0=ps[:, 6 + h // 4, (h % 4) * P:(h % 4 + 1) * P].rearrange(
                        "p (b d) -> p b d", b=TB), scalar=small[:, S_BS + h:S_BS + h + 1], in1=u, op0=ALU.add, op1=ALU.mult)
                m.then_inc(ya_done, 1)
                dve.wait_ge(fb_ld, 16 * l + 16)
                for tp in range(TB):
                    dve.wait_ge(y_mm, 2 * l + tp + 1)
                    v.tensor_tensor(yb[:, tp, :], ps[:, 4 + tp, :], fb_row, ALU.add).then_inc(yb_done, 1)
                dve.wait_ge(ms_done, l + 1)
                v.tensor_scalar(mstat[:, 1, :], mstat[:, 0, :], 1.0 / HALF, EPS, ALU.mult, ALU.add).then_inc(ms_in, 1)
                dve.wait_ge(ms_root, l + 1)
                step(v.reciprocal(mstat[:, 1, :], mstat[:, 2, :]))
                for b in range(TB):
                    v.tensor_scalar(uv[:, b, 0, :], uv[:, b, 0, :], mstat[:, 1, b:b + 1], None, ALU.mult)
                    m = v.tensor_scalar(yb[:, b, :], yb[:, b, :], mstat[:, 1, 2 + b:3 + b], None, ALU.mult)
                m.then_inc(yn_done, 1)
                for c in range(CB):
                    if c % 4 == 0:
                        dve.wait_ge(tr_mm, 2 * l + c // 4 + 1)
                    m = v.tensor_scalar(yT[:, c, :], ps[:, c // 2, (c % 2) * T:(c % 2 + 1) * T],
                                        small[:, S_GAIN + c:S_GAIN + c + 1], None, ALU.mult)
                m.then_inc(yt_done, 1)

                def residual(n, y):
                    for k in range(KC):
                        g = (3 * n + 2) * KC + k
                        m = v.scalar_tensor_tensor(out=xT[:, k, :], in0=y[:, k, :], scalar=modT[:, g:g + 1],
                                                   in1=xT[:, k, :], op0=ALU.mult, op1=ALU.add)
                    m.then_inc(x_done, 1)

                dve.wait_ge(out_mm, l + 1)
                residual(0, ps_o)
                norm(l, 1, 0)
                for b in range(TB):
                    dve.wait_ge(s_done, 2 * l + b + 1)
                    dve.sem_inc(dve_held, 1)
                    lrow = left.rearrange("p (r n) -> p r n", r=ROWS)

                    def top16(n, src, rest, val, idx):
                        for half in range(2):
                            k8 = slice(8 * half, 8 * half + 8)
                            for r in range(n):
                                m = v.max(val[:, r, k8], (src, rest)[half][:, r, :])
                            step(m, hold=True)
                            for r in range(n):
                                m = v.max_index(idx[:, r, k8], val[:, r, k8], (src, rest)[half][:, r, :])
                                if half == 0:
                                    m = v.match_replace(rest[:, r, :], val[:, r, k8], src[:, r, :], NEG)
                            step(m, hold=True)

                    top16(ROWS, scores[:, b], lrow, top_v, top_iu)
                    step(v.tensor_copy(top_i.rearrange("p h s k -> p (h s k)"), top_iu.rearrange("p r k -> p (r k)")))
                    vals = top_v.rearrange("p (h s) k -> p h s k", s=2)
                    grid = [P, HEADS, TOPK, TOPK]
                    step(v.tensor_tensor(cand.rearrange("p (h a b) -> p h a b", h=HEADS, a=TOPK),
                                         vals[:, :, 0, :].unsqueeze(3).to_broadcast(grid),
                                         vals[:, :, 1, :].unsqueeze(2).to_broadcast(grid), ALU.add), hold=True)
                    crow = cand.rearrange("p (h n) -> p h n", h=HEADS)
                    rrow = left.rearrange("p (h n) -> p h n", h=HEADS)
                    picku = pick_u.rearrange("p (h k) -> p h k", h=HEADS)
                    top16(HEADS, crow, rrow, pick_v, picku)
                    v.tensor_scalar(half_u[:, 0, :], pick_u, 4, None, ALU.logical_shift_right)
                    step(v.tensor_scalar(half_u[:, 1, :], pick_u, TOPK - 1, None, ALU.bitwise_and))
                    step(v.tensor_copy(half_f, half_u))
                    eqv = eq.rearrange("p (h k j) -> p h k j", h=HEADS, k=TOPK)
                    eqm = eq.rearrange("p (m j) -> p m j", j=TOPK)
                    for s in range(2):
                        step(v.tensor_tensor(eqm, half_f[:, s, :].unsqueeze(2).to_broadcast([P, P, TOPK]),
                                             iota[:, 0:TOPK].unsqueeze(1).to_broadcast([P, P, TOPK]), ALU.is_equal))
                        step(v.tensor_tensor(eqv, eqv, top_i[:, :, s, :].unsqueeze(2).to_broadcast(grid), ALU.mult))
                        step(v.tensor_reduce(picks[:, b, s, :], eqm, AX.X, ALU.add))
                    gate = picks[:, b, 2, :].rearrange("p (h k) -> p h k", h=HEADS)
                    hk = [P, HEADS, TOPK]
                    v.tensor_tensor(gate, pick_v, pick_v[:, :, 0:1].to_broadcast(hk), ALU.subtract).then_inc(exp_in, 1)
                    dve.wait_ge(exp_done, 2 * l + b + 1)
                    step(v.tensor_reduce(gsum[:, 0, :], gate, AX.X, ALU.add))
                    step(v.reciprocal(gsum[:, 1, :], gsum[:, 0, :]))
                    v.tensor_tensor(gate, gate, gsum[:, 1, :].unsqueeze(2).to_broadcast(hk), ALU.mult)\
                        .then_inc(picks_done, 1)
                for b in range(TB):
                    dve.wait_ge(kt_mm, 2 * l + b + 1)
                    v.tensor_copy(kT[:, :, b * P:(b + 1) * P], ps[:, 4 + b, 0:3 * P].rearrange("p (i t) -> p i t", i=3))\
                        .then_inc(kt_done, 1)
                dve.wait_ge(kt_done, 2 * l + 2)
                dve.sem_inc(hot_free, 2)
                dve.sem_inc(g_free, 2)

                def build_hot(n):
                    for j in range(GT):
                        if j % OT == 0:
                            dve.wait_ge(hot_free, l * (T // OT + 2) + 2 * n + j // OT + 1)
                        t = bass.ds(n * GT + j, 1)
                        v.tensor_scalar(hot1[:, j, :], iota, kT[:, 0, t], kT[:, 2, t], ALU.is_equal, ALU.mult)
                        m = v.tensor_scalar(hot2[:, j, :], iota, kT[:, 1, t], None, ALU.is_equal)
                        if j % OT == OT - 1:
                            m.then_inc(hot_ready, 1)

                acts = big.rearrange("p (n t) -> p n t", t=T)

                def gated(n, odd):
                    dve.wait_ge(hot_free, l * (T // OT + 2) + 2 + 2 * n + 2)
                    a = acts[:, :, bass.ds(n * GT, GT)]
                    v.tensor_tensor(a, a, ps[:, 4 + 2 * odd:6 + 2 * odd, :].rearrange("p b (t n) -> p n (b t)", n=P),
                                    ALU.mult).then_inc(g_free, 1)

                build_hot(0)
                dve.wait_ge(p_done, l + 1)
                dve.sem_inc(dve_held, 1)
                with dve.Fori(0, GROUPS // 2 - 1) as i:
                    build_hot(2 * i + 1)
                    gated(2 * i, 0)
                    build_hot(2 * i + 2)
                    gated(2 * i + 1, 1)
                build_hot(GROUPS - 1)
                gated(GROUPS - 2, 0)
                gated(GROUPS - 1, 1)
                dve.wait_ge(tile_free, SLOTS + (l + 1) * TILES)
                residual(1, ps_v)
                assert k_step[0] == DVE_STEPS, k_step[0]
            dve.wait_ge(fin_mm, 1)
            v.tensor_scalar(rstd[:, 0, :], ps[:, 6, 0:T], 1.0 / D, EPS, ALU.mult, ALU.add).then_inc(fin_in, 1)
            dve.wait_ge(fin_root, 1)
            v.reciprocal(rstd[:, 0, :], rstd[:, 1, :]).then_inc(dve_step, 1)
            dve.wait_ge(dve_step, LAYERS * DVE_STEPS + 1)
            v.tensor_tensor(hT[:], xT[:], rstd[:, 0, :].unsqueeze(1).to_broadcast([P, KC, T]), ALU.mult)\
                .then_inc(dve_step, 1)
            dve.wait_ge(dve_step, LAYERS * DVE_STEPS + 2)
            for k in range(KC):
                m = v.tensor_scalar(hT[:, k, :], hT[:, k, :], final_g[:, k:k + 1], None, ALU.mult)
            m.then_inc(fin_done, 1)


def columns(a):
    a = a.reshape(*a.shape[:-1], -1, P)
    return np.swapaxes(a, -1, -2)


def constants():
    out = np.zeros((P, N_CONST), np.float32)
    out[:, C_ID:C_ID + P] = np.eye(P)
    out[:, C_IOTA:C_IOTA + P] = np.arange(P)
    out[:, C_ONES:C_ONES + P] = 1.0
    d = np.arange(HD)
    angle = 2 * np.pi * (np.outer(d, d) % HD) / HD
    pair = np.eye(2)
    out[:, C_COSD:C_COSD + P] = np.kron(pair, np.cos(angle)) / np.sqrt(HD)
    out[:, C_SIND:C_SIND + P] = -np.kron(pair, np.sin(angle)) / np.sqrt(HD)
    s = np.arange(T)
    angle = 2 * np.pi * (np.outer(s, s) % T) / T
    for at, f in ((C_COSS, np.cos), (C_SINS, np.sin)):
        m = (f(angle) / np.sqrt(T)).reshape(TB, P, T).transpose(1, 0, 2)
        out[:, at:at + TB * T] = m.reshape(P, TB * T)
    return out


def tiles(a):
    l, n = a.shape[:2]
    return a.reshape(l, n // PER_DMA, PER_DMA, P, D).transpose(0, 1, 3, 2, 4).reshape(l, n // PER_DMA, P, PER_DMA * D)


def kernel(**inputs):
    import concourse.bacc as bacc
    from concourse.bass_utils import run_bass_kernel_spmd

    a = {k: np.asarray(v) for k, v in inputs.items()}
    L = LAYERS
    arrays = {}
    arrays["x_in"] = columns(a["x"][0]).transpose(1, 2, 0)
    arrays["c_in"] = columns(a["c"][0])
    arrays["consts_in"] = constants()
    arrays["small_in"] = np.concatenate([
        columns(a["norm1_g"]), columns(a["norm2_g"]),
        columns(np.concatenate([a["gain_a"], a["gain_b"]], -1)),
        a["gmlp_bs"].transpose(0, 2, 1),
        columns(a["mod_b"]),
        a["fnet_w"].reshape(L, PAIRS, P, HD).transpose(0, 2, 1, 3).reshape(L, P, PAIRS * HD),
        a["gmlp_ws"].transpose(0, 3, 1, 2).reshape(L, P, HEADS * P)], -1)
    arrays["fb_in"] = a["fnet_b"].reshape(L, HALF)
    keys = np.stack([a["peer_k1"], a["peer_k2"]], 2)
    arrays["keys_in"] = keys.transpose(0, 4, 1, 2, 3).reshape(L, P, ROWS, KEYS)
    for name, key in (("w_in_in", "w_in"), ("w_out_in", "w_out"), ("wq_in", "peer_wq")):
        w = a[key]
        arrays[name] = w.reshape(L, KC, P, w.shape[-1]).transpose(0, 2, 1, 3)
    arrays["mod_in"] = tiles(a["mod_w"].reshape(L, KC, P, MODS, P).transpose(0, 3, 2, 1, 4).reshape(L, MODS, P, D))
    u = a["peer_u"].reshape(L, KEYS, CHUNKS, KC, P).transpose(0, 2, 4, 3, 1)
    arrays["u_in"] = tiles(u.reshape(L, CHUNKS, P, D))
    arrays["v_in"] = tiles(a["peer_v"].reshape(L, KEYS, CHUNKS, D).transpose(0, 2, 1, 3))
    arrays["final_in"] = columns(a["final_g"])
    arrays = {k: np.ascontiguousarray(v) for k, v in arrays.items()}

    nc = bacc.Bacc("TRN2", target_bir_lowering=False, num_devices=1)
    aps = {k: nc.dram_tensor(k, v.shape, F32, kind="ExternalInput").ap() for k, v in arrays.items()}
    out = nc.dram_tensor("out", (P, KC, T), F32, kind="ExternalOutput").ap()
    build(nc, **aps, out=out)
    r = run_bass_kernel_spmd(nc, [arrays], core_ids=[0])
    y = r.results[0]["out"]
    return np.ascontiguousarray(y.transpose(2, 1, 0).reshape(1, T, D))
```

```python
from contextlib import ExitStack

import numpy as np

import concourse.bass as bass
from concourse import mybir

F32 = mybir.dt.float32
F32R = mybir.dt.float32r
U32 = mybir.dt.uint32
BF16 = mybir.dt.bfloat16
ALU = mybir.AluOpType
ACT = mybir.ActivationFunctionType
AX = mybir.AxisListType

P = 128
D = 1024
T = 256
LAYERS = 2
KC = D // P
TB = T // P
HEADS = 8
HD = 64
HALF = HEADS * HD
IN_COLS = 3 * HALF
CB = D // P
PAIRS = HALF // P
EPS = 1e-6
KEYS = 128
TOPK = 16
ROWS = 2 * HEADS
QCOLS = ROWS * P
CHUNKS = KEYS
N_MOD = 6
MODS = N_MOD * KC
NEG = -3.0e38

SLOTS = 4
PER_DMA = 2
QUEUES = SLOTS // PER_DMA
MOD_ROUNDS = MODS // SLOTS
EXP_ROUNDS = CHUNKS // SLOTS
ROUNDS = MOD_ROUNDS + 2 * EXP_ROUNDS
TILES = ROUNDS * SLOTS
HALF_CHUNKS = CHUNKS // 2
HALF_ROUNDS = EXP_ROUNDS // 2
GATE_ROUNDS = 2
AHEAD = 2

GT = 8
OT = 4
GROUPS = T // GT
HOTS = T // OT
PBANKS = 4

C_ID, C_IOTA, C_ONES, C_COSD, C_SIND = (i * P for i in range(5))
C_COSS = 5 * P
C_SINS = C_COSS + TB * T
N_CONST = C_SINS + TB * T
S_NORM1, S_NORM2, S_GAIN, S_BS, S_MODB = 0, 8, 16, 24, 32
S_FW = S_MODB + MODS
S_WS = S_FW + PAIRS * HD
N_SMALL = S_WS + HEADS * P


def build(nc, x_in, c_in, consts_in, small_in, fb_in, keys_in, w_in_in, w_out_in, wq_in, mod_in, u_in, v_in,
          final_in, out):
    ctx = ExitStack()
    with ctx:
        def sb(name, shape, dt=F32):
            return ctx.enter_context(nc.sbuf_tensor(name, shape, dt))

        def sem(name):
            return ctx.enter_context(nc.semaphore(name))

        big = sb("expert_acts", [P, CHUNKS * T])
        xT = sb("xT", [P, KC, T])
        h_hi = sb("h_hi", [P, KC, T], F32R)
        h_lo = sb("h_lo", [P, KC, T], F32R)
        ring = sb("ring", [P, SLOTS, D])
        t_hi = sb("tile_hi", [P, AHEAD, D], F32R)
        t_lo = sb("tile_lo", [P, AHEAD, D], F32R)
        w_hi = sb("w_hi", [P, AHEAD, T], F32R)
        w_lo = sb("w_lo", [P, AHEAD, T], F32R)
        small = sb("small", [P, N_SMALL])
        consts = sb("consts", [P, N_CONST])
        kT = sb("routed", [P, 3, T])
        hot2 = sb("hot2", [P, 2 * OT, HD])
        modT = sb("modT", [P, MODS])
        ab = sb("ab", [P, 2, KC])
        cT = sb("cT", [P, KC])
        siluT = sb("siluT", [P, KC])
        final_g = sb("final_g", [P, KC])
        rstd = sb("rstd", [P, T])
        stat = sb("stat", [P, 4, ROWS])
        mstat = sb("mstat", [P, 3, 4])
        zeros = sb("zeros", [P, P], BF16)

        w_in_sb = big[:, 0:KC * IN_COLS].rearrange("p (k n) -> p k n", k=KC)
        FB_AT = KC * IN_COLS
        fblock = big[:, FB_AT:FB_AT + PAIRS * 256].rearrange("p (r s g e) -> p r s g e", r=PAIRS, s=2, g=2)
        fb_row = big[:, FB_AT + 1024:FB_AT + 1024 + HALF]
        wq_sb = big[:, 0:KC * QCOLS].rearrange("p (k n) -> p k n", k=KC)
        h1T = big[:, FB_AT + 2048:FB_AT + 4096].rearrange("p (k t) -> p k t", k=KC)
        M0 = KC * QCOLS
        uv = big[:, M0:M0 + 2048].rearrange("p (b s n) -> p b s n", b=TB, s=2)
        zfT = big[:, M0 + 2048:M0 + 3072].rearrange("p (r t) -> p r t", r=PAIRS)
        rt = big[:, M0 + 3072:M0 + 5120].rearrange("p (b s n) -> p b s n", b=TB, s=2)
        yb = big[:, M0 + 5120:M0 + 6144].rearrange("p (b n) -> p b n", b=TB)
        yT = big[:, M0 + 6144:M0 + 8192].rearrange("p (c t) -> p c t", c=CB)
        sqv = yT
        w_out_sb = big[:, M0 + 8192:M0 + 16384].rearrange("p (c n) -> p c n", c=CB)
        qT = big[:, M0:M0 + 4096].rearrange("p (r t) -> p r t", r=ROWS)
        scores = big[:, M0 + 4096:M0 + 8192].rearrange("p (b r n) -> p b r n", b=TB, r=ROWS)
        h2T = big[:, M0 + 4096:M0 + 6144].rearrange("p (k t) -> p k t", k=KC)
        keys = big[:, M0 + 8192:M0 + 10240].rearrange("p (r n) -> p r n", r=ROWS)
        left = big[:, M0 + 10240:M0 + 12288]
        cand = big[:, M0 + 12288:M0 + 14336]
        eq = big[:, M0 + 14336:M0 + 16384]
        at = [M0]

        def scratch(n, dt=F32):
            a = big[:, at[0]:at[0] + n]
            at[0] += n
            return a if dt == F32 else a.bitcast(dt)

        top_v = scratch(ROWS * TOPK).rearrange("p (r k) -> p r k", r=ROWS)
        top_iu = scratch(ROWS * TOPK, U32).rearrange("p (r k) -> p r k", r=ROWS)
        top_i = scratch(ROWS * TOPK).rearrange("p (h s k) -> p h s k", h=HEADS, s=2)
        pick_v = scratch(P).rearrange("p (h k) -> p h k", h=HEADS)
        pick_u = scratch(P, U32)
        half_u = scratch(2 * P, U32).rearrange("p (s n) -> p s n", s=2)
        half_f = scratch(2 * P).rearrange("p (s n) -> p s n", s=2)
        picks = scratch(TB * 3 * P).rearrange("p (b s n) -> p b s n", b=TB, s=3)
        gsum = scratch(2 * HEADS).rearrange("p (s h) -> p s h", s=2)
        assert at[0] <= M0 + 4096

        hot1 = small[:, S_WS:S_WS + 2 * OT * P].rearrange("p (o n) -> p o n", o=2 * OT)

        ident = consts[:, C_ID:C_ID + P]
        iota = consts[:, C_IOTA:C_IOTA + P]
        ones = consts[:, C_ONES:C_ONES + P]

        ps = ctx.enter_context(nc.psum_tensor("ps", [P, 8, 512], F32))
        ps_v = ps[:, 0:4, :].rearrange("p b (h t) -> p (b h) t", h=2)
        ps_o = ps[:, 4:8, :].rearrange("p b (h t) -> p (b h) t", h=2)

        once = sem("once_loaded")
        small_ld, keys_ld, fb_ld = sem("small_loaded"), sem("keys_loaded"), sem("fb_loaded")
        win_ld, wout_ld, wq_ld = sem("w_in_loaded"), sem("w_out_loaded"), sem("wq_loaded")
        ring_full = [sem(f"ring_full{q}") for q in range(QUEUES)]
        tile_free = sem("tile_free")
        hi_ready = sem("hi_ready")
        whi_ready, wlo_ready = sem("whi_ready"), sem("wlo_ready")
        tile_mm = sem("tile_mm")
        hs_in, hs_done = sem("h_hi_done"), sem("h_lo_done")
        root_in, ms_in, fin_in = sem("root_in"), sem("ms_in"), sem("fin_in")
        silu_done = sem("silu_done")
        sq_done, sum_mm, root_done = sem("sq_done"), sem("sum_mm"), sem("root_done")
        h_done = sem("h_done")
        fw_mm, fw_done = sem("fw_mm"), sem("fw_done")
        z_mm, gelu_done, zf_done = sem("z_mm"), sem("gelu_done"), sem("zf_done")
        ln_var, ln_root, ln_done = sem("ln_var"), sem("ln_root"), sem("ln_done")
        sv_mm, ya_done = sem("sv_mm"), sem("ya_done")
        rt_mm, rt_done = sem("rt_mm"), sem("rt_done")
        y_mm, yb_done = sem("y_mm"), sem("yb_done")
        ms_done, ms_root, yn_done = sem("ms_done"), sem("ms_root"), sem("yn_done")
        tr_mm, yt_done = sem("tr_mm"), sem("yt_done")
        out_mm, x_done = sem("out_mm"), sem("x_done")
        q_mm, q_done = sem("q_mm"), sem("q_done")
        s_mm, s_done = sem("s_mm"), sem("s_done")
        exp_in, exp_done = sem("exp_in"), sem("exp_done")
        picks_done, kt_mm, kt_done = sem("picks_done"), sem("kt_mm"), sem("kt_done")
        p_free = sem("p_free")
        hot1_ready, hot2_ready, hot_free = sem("hot1_ready"), sem("hot2_ready"), sem("hot_free")
        g_free = sem("g_free")
        act_step = sem("act_step")
        dve_step = sem("dve_step")
        zeros_done = sem("zeros_done")
        dve_held, pe_held = sem("dve_held"), sem("pe_held")
        fin_sq, fin_mm, fin_root, fin_done = sem("fin_sq"), sem("fin_mm"), sem("fin_root"), sem("fin_done")
        out_st = sem("out_stored")
        DVE_STEPS = 184

        block = ctx.enter_context(nc.Block())

        @block.sync
        def _(sp):
            def stream(l, first, rounds, src):
                with sp.Fori(0, rounds) as r:
                    for q in range(QUEUES):
                        sp.wait_ge(tile_free, (l * ROUNDS + first + r) * SLOTS + (q + 1) * PER_DMA)
                        sp.dma_start(ring[:, q * PER_DMA:(q + 1) * PER_DMA, :],
                                     src[bass.ds(l, 1), bass.ds(r * QUEUES + q, 1)].rearrange(
                                         "a b p (s n) -> (a b p) s n", s=PER_DMA)).then_inc(ring_full[q], 16)

            with sp.Fori(0, LAYERS) as l:
                stream(l, 0, MOD_ROUNDS, mod_in)
                stream(l, MOD_ROUNDS, EXP_ROUNDS, u_in)
                stream(l, MOD_ROUNDS + EXP_ROUNDS, EXP_ROUNDS, v_in)
            sp.wait_ge(fin_done, 1)
            sp.dma_start(out, h1T).then_inc(out_st, 16)
            sp.wait_ge(out_st, 16)

        @block.gpsimd
        def _(pool):
            pool.dma_start(cT[:], c_in).then_inc(once, 16)
            pool.dma_start(xT[:], x_in).then_inc(once, 16)
            pool.dma_start(consts[:], consts_in).then_inc(once, 16)
            pool.dma_start(final_g[:], final_in).then_inc(once, 16)
            with pool.Fori(0, LAYERS) as l:
                pool.wait_ge(x_done, 2 * l + 1)
                pool.dma_start(small[:], small_in[bass.ds(l, 1)].rearrange("a p n -> (a p) n")).then_inc(small_ld, 16)
                pool.dma_start(w_in_sb, w_in_in[bass.ds(l, 1)].rearrange("a p k n -> (a p) k n")).then_inc(win_ld, 16)
                pool.dma_start(fb_row, fb_in[bass.ds(l, 1)].to_broadcast([P, HALF])).then_inc(fb_ld, 16)
                pool.dma_start(w_out_sb, w_out_in[bass.ds(l, 1)].rearrange("a p k n -> (a p) k n")).then_inc(wout_ld, 16)
                pool.wait_ge(z_mm, 8 * l + 8)
                pool.wait_ge(rt_mm, 2 * l + 2)
                pool.wait_ge(yb_done, 2 * l + 2)
                pool.dma_start(wq_sb, wq_in[bass.ds(l, 1)].rearrange("a p k n -> (a p) k n")).then_inc(wq_ld, 16)
                pool.wait_ge(out_mm, l + 1)
                pool.dma_start(keys, keys_in[bass.ds(l, 1)].rearrange("a p k n -> (a p) k n")).then_inc(keys_ld, 16)

        @block.tensor
        def _(pe):
            def mm(out, lhsT, rhs, start, stop):
                return nc.tensor.matmul(out, lhsT, rhs, start=start, stop=stop, skip_group_check=True)

            def column_sums(bank, sq):
                for k in range(KC):
                    m = mm(ps[:, bank, 0:T], ones, sq[:, k, :], k == 0, k == KC - 1)
                return m

            pe.sem_inc(tile_free, SLOTS)
            pe.wait_ge(once, 64)
            pe.wait_ge(silu_done, 1)
            pe.wait_ge(zeros_done, 1)
            with pe.Fori(0, LAYERS) as l:
                with pe.Fori(0, MOD_ROUNDS) as r:
                    for s in range(SLOTS):
                        if s % PER_DMA == 0:
                            pe.wait_ge(ring_full[s // PER_DMA], 16 * (l * ROUNDS + r + 1))
                        for k in range(KC):
                            m = mm(ps[:, 7, bass.ds(r * SLOTS + s, 1)], ring[:, s, k * P:(k + 1) * P],
                                   siluT[:, k:k + 1], k == 0, k == KC - 1)
                        m.then_inc(tile_free, 1)
                pe.wait_ge(small_ld, 16 * l + 16)
                mm(ps[:, 5, 0:256], consts[:, C_COSD:C_COSD + P], small[:, S_FW:S_FW + 256], True, True)
                mm(ps[:, 5, 256:512], consts[:, C_SIND:C_SIND + P], small[:, S_FW:S_FW + 256], True, True)\
                    .then_inc(fw_mm, 1)
                pe.wait_ge(sq_done, 2 * l + 1)
                column_sums(6, h1T).then_inc(sum_mm, 1)
                pe.wait_ge(h_done, 2 * l + 1)
                pe.wait_ge(win_ld, 16 * l + 16)
                for s in range(2):
                    for b in range(TB):
                        for k in range(KC):
                            m = mm(ps[:, 2 * b + (1 - s), :], h1T[:, k, b * P:(b + 1) * P],
                                   w_in_sb[:, k, (1 - s) * HALF:(2 - s) * HALF], k == 0, k == KC - 1)
                        m.then_inc(z_mm, 1)
                pe.wait_ge(fw_done, l + 1)
                for r in range(PAIRS):
                    for k in range(KC):
                        m = mm(ps[:, 4 + r // 2, (r % 2) * T:(r % 2 + 1) * T],
                               w_in_sb[:, k, 2 * HALF + r * P:2 * HALF + (r + 1) * P], h1T[:, k, :],
                               k == 0, k == KC - 1)
                    m.then_inc(z_mm, 1)
                pe.wait_ge(ln_done, l + 1)
                for h in range(HEADS):
                    m = mm(ps[:, 6 + h // 4, (h % 4) * P:(h % 4 + 1) * P], small[:, S_WS + h * P:S_WS + (h + 1) * P],
                           uv[:, :, 1, h * HD:(h + 1) * HD], True, True)
                m.then_inc(sv_mm, 1)
                pe.wait_ge(zf_done, 2 * l + 2)
                pe.wait_ge(gelu_done, 4 * l + 4)
                for b in range(TB):
                    for r in range(PAIRS):
                        m = mm(ps[:, 2 * b + r // 2, (r % 2) * 256:(r % 2 + 1) * 256], zfT[:, r, b * P:(b + 1) * P],
                               fblock[:, r].rearrange("p s g e -> p (s g e)"), True, True)
                    m.then_inc(rt_mm, 1)
                pe.wait_ge(rt_done, 2 * l + 2)
                for tp in range(TB):
                    n = 0
                    for b in range(TB):
                        for s, at_ in enumerate((C_COSS, C_SINS)):
                            m = mm(ps[:, 4 + tp, :], consts[:, at_ + b * T + tp * P:at_ + b * T + (tp + 1) * P],
                                   rt[:, b, s, :], n == 0, n == 2 * TB - 1)
                            n += 1
                    m.then_inc(y_mm, 1)
                pe.wait_ge(yn_done, l + 1)
                for g in range(2):
                    for c in range(CB // 2):
                        for b in range(TB):
                            src = uv[:, b, 0, c * P:(c + 1) * P] if g == 0 else yb[:, b, c * P:(c + 1) * P]
                            m = nc.tensor.transpose(ps[:, 2 * g + c // 2, (c % 2) * T + b * P:(c % 2) * T + (b + 1) * P],
                                                    src, ident)
                    m.then_inc(tr_mm, 1)
                pe.wait_ge(yt_done, l + 1)
                pe.wait_ge(wout_ld, 16 * l + 16)
                for d in range(KC):
                    for c in range(CB):
                        m = mm(ps_o[:, d, :], w_out_sb[:, c, d * P:(d + 1) * P], yT[:, c, :], c == 0, c == CB - 1)
                m.then_inc(out_mm, 1)
                pe.wait_ge(sq_done, 2 * l + 2)
                column_sums(0, h2T).then_inc(sum_mm, 1)
                pe.wait_ge(h_done, 2 * l + 2)
                pe.wait_ge(wq_ld, 16 * l + 16)
                for r in range(ROWS):
                    for k in range(KC):
                        m = mm(ps[:, r // 2, (r % 2) * T:(r % 2 + 1) * T], wq_sb[:, k, r * P:(r + 1) * P], h2T[:, k, :],
                               k == 0, k == KC - 1)
                    if r % 2:
                        m.then_inc(q_mm, 1)
                pe.wait_ge(keys_ld, 16 * l + 16)
                for b in range(TB):
                    pe.wait_ge(q_done, 8 * l + 8)
                    for r in range(ROWS):
                        m = mm(ps[:, 4 - 4 * b + r // 4, (r % 4) * P:(r % 4 + 1) * P], qT[:, r, b * P:(b + 1) * P],
                               keys[:, r, :], True, True)
                    m.then_inc(s_mm, 1)

                def split_mm(out, a_hi, a_lo, b_hi, b_lo, start, stop):
                    mm(out, a_hi, b_hi, start, False)
                    mm(out, a_hi, b_lo, False, False)
                    return mm(out, a_lo, b_hi, False, stop)

                def expert_in(r, s):
                    pe.wait_ge(tile_free, SLOTS + l * TILES + MODS + r * SLOTS + s + 1)
                    pe.wait_ge(p_free, l * CHUNKS + r * SLOTS + s + 1)
                    for k in range(KC):
                        col = slice(k * P, (k + 1) * P)
                        m = split_mm(ps[:, s % PBANKS, 0:T], t_hi[:, s % AHEAD, col], t_lo[:, s % AHEAD, col],
                                     h_hi[:, k, :], h_lo[:, k, :], k == 0, k == KC - 1)
                    m.then_inc(tile_mm, 1)

                def expert_out(r, s):
                    pe.wait_ge(tile_free, SLOTS + l * TILES + MODS + CHUNKS + r * SLOTS + s + 1)
                    pe.wait_ge(wlo_ready, l * CHUNKS + r * SLOTS + s + 1)
                    for d in range(KC):
                        col = slice(d * P, (d + 1) * P)
                        m = split_mm(ps_v[:, d, :], t_hi[:, s % AHEAD, col], t_lo[:, s % AHEAD, col],
                                     w_hi[:, s % AHEAD, :], w_lo[:, s % AHEAD, :], False, False)
                    m.then_inc(tile_mm, 1)

                def scatter(half, i, s):
                    n = half * HOTS + i * SLOTS + s
                    pe.wait_ge(hot1_ready, l * 2 * HOTS + n + 1)
                    pe.wait_ge(hot2_ready, l * 2 * HOTS + n + 1)
                    if s % 2 == 0:
                        pe.wait_ge(g_free, l * 2 * GROUPS + half * GROUPS + i * 2 + s // 2 + 1)
                    for t in range(OT):
                        o = (s % 2) * OT + t
                        m = mm(ps[:, 4 + s // 2, o * HD:(o + 1) * HD], hot1[:, o, :], hot2[:, o, :], True, True)
                    m.then_inc(hot_free, 1)

                pe.wait_ge(s_done, 2 * l + 2)
                pe.wait_ge(hs_done, 2 * l + 2)
                pe.sem_inc(pe_held, 1)
                with pe.Fori(0, HALF_ROUNDS - 1) as r:
                    for s in range(SLOTS):
                        expert_in(r, s)
                for b in range(TB):
                    pe.wait_ge(picks_done, 2 * l + b + 1)
                    for i in range(3):
                        m = nc.tensor.transpose(ps[:, 6 + b, i * P:(i + 1) * P], picks[:, b, i, :], ident)
                    m.then_inc(kt_mm, 1)
                for s in range(SLOTS):
                    expert_in(HALF_ROUNDS - 1, s)
                with pe.Fori(0, HALF_ROUNDS) as i:
                    for s in range(SLOTS):
                        expert_in(i + HALF_ROUNDS, s)
                        scatter(0, i, s)
                pe.wait_ge(p_free, PBANKS + (l + 1) * CHUNKS)
                for b in range(4):
                    mm(ps[:, b, :], zeros[:], consts[:, 0:256].bitcast(BF16), True, False)
                with pe.Fori(0, HALF_ROUNDS) as i:
                    for s in range(SLOTS):
                        expert_out(i, s)
                        scatter(1, i, s)
                with pe.Fori(HALF_ROUNDS, EXP_ROUNDS) as i:
                    for s in range(SLOTS):
                        expert_out(i, s)
            pe.wait_ge(fin_sq, 1)
            column_sums(6, h1T).then_inc(fin_mm, 1)

        @block.scalar
        def _(act):
            act.wait_ge(once, 64)
            nc.scalar.activation(siluT[:], cT[:], ACT.Silu).then_inc(silu_done, 1)
            with act.Fori(0, LAYERS) as l:
                act.wait_ge(x_done, 2 * l + 1)
                nc.scalar.activation(h1T, xT[:], ACT.Square).then_inc(sq_done, 1)
                act.wait_ge(root_in, 2 * l + 1)
                nc.scalar.activation(rstd[:], rstd[:], ACT.Sqrt).then_inc(root_done, 1)
                for s in range(2):
                    for b in range(TB):
                        act.wait_ge(z_mm, 8 * l + 2 * s + b + 1)
                        nc.scalar.activation(uv[:, b, 1 - s, :], ps[:, 2 * b + (1 - s), :], ACT.Gelu).then_inc(gelu_done, 1)
                act.wait_ge(ln_var, l + 1)
                nc.scalar.activation(stat[:, 3, :], stat[:, 2, :], ACT.Sqrt).then_inc(ln_root, 1)
                for b in range(TB):
                    act.wait_ge(rt_mm, 2 * l + b + 1)
                    src = ps[:, 2 * b:2 * b + 2, :].rearrange("p c (r s n) -> p (c r) s n", r=2, s=2)
                    nc.scalar.activation(rt[:, b].rearrange("p s (r n) -> p r s n", r=PAIRS), src, ACT.Copy)\
                        .then_inc(rt_done, 1)
                act.wait_ge(ya_done, l + 1)
                act.wait_ge(y_mm, 2 * l + 2)
                for b in range(TB):
                    nc.scalar.activation(rt[:, b, 0, :], uv[:, b, 0, :], ACT.Square, accum_out=mstat[:, 0, b:b + 1])
                act.wait_ge(yb_done, 2 * l + 2)
                for b in range(TB):
                    m = nc.scalar.activation(rt[:, b, 1, :], yb[:, b, :], ACT.Square, accum_out=mstat[:, 0, 2 + b:3 + b])
                m.then_inc(ms_done, 1)
                act.wait_ge(ms_in, l + 1)
                nc.scalar.activation(mstat[:, 2, :], mstat[:, 1, :], ACT.Sqrt).then_inc(ms_root, 1)
                act.wait_ge(x_done, 2 * l + 2)
                nc.scalar.activation(h2T, xT[:], ACT.Square).then_inc(sq_done, 1)
                act.wait_ge(root_in, 2 * l + 2)
                nc.scalar.activation(rstd[:], rstd[:], ACT.Sqrt).then_inc(root_done, 1)
                act.wait_ge(h_done, 2 * l + 2)
                for k in range(2):
                    kc = slice(k * KC // 2, (k + 1) * KC // 2)
                    nc.scalar.activation(h_hi[:, kc, :], h2T[:, kc, :], ACT.Copy).then_inc(hs_in, 1)
                for i in range(ROWS // 2):
                    act.wait_ge(q_mm, 8 * l + i + 1)
                    nc.scalar.activation(qT[:, 2 * i:2 * i + 2, :],
                                         ps[:, i, :].rearrange("p (r t) -> p r t", r=2), ACT.Copy).then_inc(q_done, 1)
                act.wait_ge(hs_done, 2 * l + 2)
                for b in range(TB):
                    act.wait_ge(s_mm, 2 * l + b + 1)
                    nc.scalar.activation(scores[:, b], ps[:, 4 - 4 * b:8 - 4 * b, :].rearrange(
                        "p c (r n) -> p (c r) n", r=4), ACT.Copy).then_inc(s_done, 1)

                def split_tile(n, s):
                    if s % PER_DMA == 0:
                        act.wait_ge(ring_full[s // PER_DMA], (l * TILES + MODS + n) * (16 // SLOTS) + (16 - 16 * s // SLOTS))
                    nc.scalar.activation(t_hi[:, s % AHEAD, :], ring[:, s, :], ACT.Copy).then_inc(hi_ready, 1)

                def next_tile(n, s):
                    act.wait_ge(tile_mm, l * 2 * CHUNKS + n + 1)
                    split_tile(n + AHEAD, (s + AHEAD) % SLOTS)

                def gelu(c, s):
                    nc.scalar.activation(big[:, bass.ds(c * T, T)], ps[:, s % PBANKS, 0:T], ACT.Gelu).then_inc(p_free, 1)

                def split_w(c, s):
                    nc.scalar.activation(w_hi[:, s % AHEAD, :], big[:, bass.ds(c * T, T)], ACT.Copy).then_inc(whi_ready, 1)

                def hot(half, n, s):
                    o = (s % 2) * OT
                    act.wait_ge(hot_free, l * 2 * HOTS + half * HOTS + n + 1)
                    for t in range(OT):
                        m = nc.scalar.activation(hot2[:, o + t, :], iota[:, half * HD:(half + 1) * HD], ACT.Abs,
                                                 bias=kT[:, 1, bass.ds(n * OT + t, 1)])
                    m.then_inc(act_step, 1)
                    act.wait_ge(act_step, l * 2 * HOTS + half * HOTS + n + 1)
                    nc.scalar.activation(hot2[:, o:o + OT, :], hot2[:, o:o + OT, :], ACT.Relu, bias=1.0, scale=-1.0)\
                        .then_inc(hot2_ready, 1)

                for s in range(AHEAD):
                    split_tile(s, s)

                def first_half(r0, r1):
                    with act.Fori(r0, r1) as r:
                        for s in range(SLOTS):
                            next_tile(r * SLOTS + s, s)
                            gelu(r * SLOTS + s, s)

                first_half(0, HALF_ROUNDS - GATE_ROUNDS)
                for b in range(TB):
                    act.wait_ge(exp_in, 2 * l + b + 1)
                    g = picks[:, b, 2, :]
                    nc.scalar.activation(g, g, ACT.Exp).then_inc(exp_done, 1)
                first_half(HALF_ROUNDS - GATE_ROUNDS, HALF_ROUNDS)

                act.wait_ge(kt_done, 2 * l + 2)
                hot(0, 0, 0)

                def in_round(i, last):
                    for s in range(SLOTS):
                        c = i * SLOTS + s + HALF_CHUNKS
                        next_tile(c, s)
                        gelu(c, s)
                        if not (last and s == SLOTS - 1):
                            hot(0, i * SLOTS + s + 1, (s + 1) % SLOTS)

                with act.Fori(0, HALF_ROUNDS - 1) as i:
                    in_round(i, False)
                in_round(HALF_ROUNDS - 1, True)

                hot(1, 0, 0)
                act.wait_ge(g_free, 2 + l * 2 * GROUPS + GROUPS)
                for s in range(AHEAD):
                    split_w(s, s)

                def out_round(half, i, last):
                    for s in range(SLOTS):
                        c = i * SLOTS + s + half * HALF_CHUNKS
                        if last and half == 1 and s >= SLOTS - AHEAD:
                            continue
                        next_tile(c + CHUNKS, s)
                        if not (last and s >= SLOTS - AHEAD):
                            split_w(c + AHEAD, (s + AHEAD) % SLOTS)
                        if half == 0 and not (last and s == SLOTS - 1):
                            hot(1, i * SLOTS + s + 1, (s + 1) % SLOTS)

                with act.Fori(0, HALF_ROUNDS - 1) as i:
                    out_round(0, i, False)
                out_round(0, HALF_ROUNDS - 1, True)
                act.wait_ge(g_free, 2 + (l + 1) * 2 * GROUPS)
                for s in range(AHEAD):
                    split_w(HALF_CHUNKS + s, s)
                with act.Fori(0, HALF_ROUNDS - 1) as i:
                    out_round(1, i, False)
                out_round(1, HALF_ROUNDS - 1, True)
            act.wait_ge(x_done, 2 * LAYERS + 1)
            nc.scalar.activation(h1T, xT[:], ACT.Square).then_inc(fin_sq, 1)
            act.wait_ge(fin_in, 1)
            nc.scalar.activation(rstd[:], rstd[:], ACT.Sqrt).then_inc(fin_root, 1)

        @block.vector
        def _(dve):
            v = nc.vector
            v.memset(zeros[:], 0.0).then_inc(zeros_done, 1)
            dve.wait_ge(once, 64)
            dve.sem_inc(x_done, 1)
            dve.sem_inc(hot_free, 2)
            dve.sem_inc(g_free, 2)
            dve.sem_inc(p_free, PBANKS)

            def norm(l, n, bank, h):
                dve.wait_ge(sum_mm, 2 * l + n + 1)
                v.tensor_scalar(rstd[:], ps[:, bank, 0:T], 1.0 / D, EPS, ALU.mult, ALU.add).then_inc(root_in, 1)
                dve.wait_ge(root_done, 2 * l + n + 1)
                step(v.reciprocal(rstd[:], rstd[:]))
                step(v.tensor_tensor(h, xT[:], rstd[:].unsqueeze(1).to_broadcast([P, KC, T]), ALU.mult))
                for k in range(KC):
                    m = v.tensor_scalar(h[:, k, :], h[:, k, :], ab[:, n, k:k + 1],
                                        modT[:, 3 * KC * n + k:3 * KC * n + k + 1], ALU.mult, ALU.add)
                m.then_inc(h_done, 1)

            with dve.Fori(0, LAYERS) as l:
                k_step = [0]

                def step(m, hold=False):
                    k_step[0] += 1
                    m.then_inc(dve_step, 1)
                    dve.wait_ge(dve_step, l * DVE_STEPS + k_step[0])
                    if hold:
                        dve.sem_inc(dve_held, 1)

                def mark(m):
                    k_step[0] += 1
                    m.then_inc(dve_step, 1)
                    return k_step[0]

                def wait_mark(k, hold=True):
                    dve.wait_ge(dve_step, l * DVE_STEPS + k)
                    if hold:
                        dve.sem_inc(dve_held, 1)

                step(v.memset(fblock, 0.0))
                dve.wait_ge(small_ld, 16 * l + 16)
                dve.wait_ge(tile_free, SLOTS + l * TILES + MODS)
                step(v.tensor_tensor(modT[:], ps[:, 7, 0:MODS], small[:, S_MODB:S_MODB + MODS], ALU.add))
                for n, at_ in enumerate((S_NORM1, S_NORM2)):
                    m = v.scalar_tensor_tensor(out=ab[:, n, :], in0=modT[:, (3 * n + 1) * KC:(3 * n + 2) * KC], scalar=1.0,
                                               in1=small[:, at_:at_ + KC], op0=ALU.add, op1=ALU.mult)
                step(m)
                dve.wait_ge(fw_mm, l + 1)
                for g in range(2):
                    half = slice(g * HD, (g + 1) * HD)
                    for s in range(2):
                        m = v.tensor_copy(fblock[half, :, s, g, :],
                                          ps[half, 5, s * 256:(s + 1) * 256].rearrange("p (r e) -> p r e", r=PAIRS))
                m.then_inc(fw_done, 1)
                norm(l, 0, 6, h1T)
                dve.wait_ge(gelu_done, 4 * l + 2)
                vh = uv[:, :, 1, :].rearrange("p b (h d) -> p b h d", h=HEADS)
                sqh = sqv[:, 0:4, :].rearrange("p c t -> p (c t)").rearrange("p (b h d) -> p b h d", b=TB, h=HEADS)

                def st(i):
                    return stat[:, i, :].rearrange("p (b h) -> p b h", b=TB)

                def wide(i):
                    return st(i).unsqueeze(3).to_broadcast([P, TB, HEADS, HD])

                step(v.tensor_reduce(st(0), vh, AX.X, ALU.add))
                step(v.tensor_scalar(stat[:, 1, :], stat[:, 0, :], -1.0 / HD, None, ALU.mult))
                step(v.tensor_tensor(vh, vh, wide(1), ALU.add))
                step(v.tensor_tensor(sqh, vh, vh, ALU.mult))
                step(v.tensor_reduce(st(0), sqh, AX.X, ALU.add))
                v.tensor_scalar(stat[:, 2, :], stat[:, 0, :], 1.0 / HD, EPS, ALU.mult, ALU.add).then_inc(ln_var, 1)
                dve.wait_ge(ln_root, l + 1)
                step(v.reciprocal(stat[:, 1, :], stat[:, 3, :]))
                v.tensor_tensor(vh, vh, wide(1), ALU.mult).then_inc(ln_done, 1)
                for i in range(2):
                    dve.wait_ge(z_mm, 8 * l + 6 + 2 * i)
                    v.tensor_copy(zfT[:, 2 * i:2 * i + 2, :], ps[:, 4 + i, :].rearrange("p (r t) -> p r t", r=2))\
                        .then_inc(zf_done, 1)
                dve.wait_ge(sv_mm, l + 1)
                dve.wait_ge(gelu_done, 4 * l + 4)
                for h in range(HEADS):
                    u = uv[:, :, 0, h * HD:(h + 1) * HD]
                    m = v.scalar_tensor_tensor(out=u, in0=ps[:, 6 + h // 4, (h % 4) * P:(h % 4 + 1) * P].rearrange(
                        "p (b d) -> p b d", b=TB), scalar=small[:, S_BS + h:S_BS + h + 1], in1=u, op0=ALU.add, op1=ALU.mult)
                m.then_inc(ya_done, 1)
                dve.wait_ge(fb_ld, 16 * l + 16)
                for tp in range(TB):
                    dve.wait_ge(y_mm, 2 * l + tp + 1)
                    v.tensor_tensor(yb[:, tp, :], ps[:, 4 + tp, :], fb_row, ALU.add).then_inc(yb_done, 1)
                dve.wait_ge(ms_done, l + 1)
                v.tensor_scalar(mstat[:, 1, :], mstat[:, 0, :], 1.0 / HALF, EPS, ALU.mult, ALU.add).then_inc(ms_in, 1)
                dve.wait_ge(ms_root, l + 1)
                step(v.reciprocal(mstat[:, 1, :], mstat[:, 2, :]))
                for b in range(TB):
                    v.tensor_scalar(uv[:, b, 0, :], uv[:, b, 0, :], mstat[:, 1, b:b + 1], None, ALU.mult)
                    m = v.tensor_scalar(yb[:, b, :], yb[:, b, :], mstat[:, 1, 2 + b:3 + b], None, ALU.mult)
                m.then_inc(yn_done, 1)
                for c in range(CB):
                    if c % 4 == 0:
                        dve.wait_ge(tr_mm, 2 * l + c // 4 + 1)
                    m = v.tensor_scalar(yT[:, c, :], ps[:, c // 2, (c % 2) * T:(c % 2 + 1) * T],
                                        small[:, S_GAIN + c:S_GAIN + c + 1], None, ALU.mult)
                m.then_inc(yt_done, 1)

                def residual(n, y):
                    for k in range(KC):
                        g = (3 * n + 2) * KC + k
                        m = v.scalar_tensor_tensor(out=xT[:, k, :], in0=y[:, k, :], scalar=modT[:, g:g + 1],
                                                   in1=xT[:, k, :], op0=ALU.mult, op1=ALU.add)
                    m.then_inc(x_done, 1)

                dve.wait_ge(out_mm, l + 1)
                residual(0, ps_o)
                norm(l, 1, 0, h2T)
                for k in range(2):
                    kc = slice(k * KC // 2, (k + 1) * KC // 2)
                    dve.wait_ge(hs_in, 2 * l + k + 1)
                    v.tensor_tensor(h_lo[:, kc, :], h2T[:, kc, :], h_hi[:, kc, :].bitcast(F32), ALU.subtract)\
                        .then_inc(hs_done, 1)
                def split_tile(n, s):
                    dve.wait_ge(hi_ready, l * 2 * CHUNKS + n + 1)
                    v.tensor_tensor(t_lo[:, s % AHEAD, :], ring[:, s, :], t_hi[:, s % AHEAD, :].bitcast(F32), ALU.subtract)\
                        .then_inc(tile_free, 1)

                done = [0]

                def split_next():
                    split_tile(done[0], done[0] % SLOTS)
                    done[0] += 1

                dve.wait_ge(s_done, 2 * l + 2)
                for _ in range(AHEAD):
                    split_next()
                dve.sem_inc(dve_held, 1)
                rest = left.rearrange("p (r n) -> p r n", r=ROWS)
                crow = cand.rearrange("p (h n) -> p h n", h=HEADS)
                crest = left.rearrange("p (h n) -> p h n", h=HEADS)
                picku = pick_u.rearrange("p (h k) -> p h k", h=HEADS)
                vals = top_v.rearrange("p (h s) k -> p h s k", s=2)
                grid = [P, HEADS, TOPK, TOPK]
                hk = [P, HEADS, TOPK]
                eqv = eq.rearrange("p (h k j) -> p h k j", h=HEADS, k=TOPK)
                eqm = eq.rearrange("p (m j) -> p m j", j=TOPK)

                def top16(src, rest, val, idx):
                    step(v.max(val[:, 0:8], src), hold=True)
                    v.max_index(idx[:, 0:8], val[:, 0:8], src)
                    m = v.match_replace(rest, val[:, 0:8], src, NEG)
                    k = mark(m)
                    split_next()
                    wait_mark(k)
                    step(v.max(val[:, 8:16], rest), hold=True)
                    return v.max_index(idx[:, 8:16], val[:, 8:16], rest)

                for b in range(TB):
                    for r in range(ROWS):
                        m = top16(scores[:, b, r, :], rest[:, r, :], top_v[:, r, :], top_iu[:, r, :])
                    step(m)
                    v.tensor_copy(top_i.rearrange("p h s k -> p (h s k)"), top_iu.rearrange("p r k -> p (r k)"))
                    k = mark(v.tensor_tensor(cand.rearrange("p (h a b) -> p h a b", h=HEADS, a=TOPK),
                                             vals[:, :, 0, :].unsqueeze(3).to_broadcast(grid),
                                             vals[:, :, 1, :].unsqueeze(2).to_broadcast(grid), ALU.add))
                    split_next()
                    wait_mark(k)
                    for h in range(HEADS):
                        m = top16(crow[:, h, :], crest[:, h, :], pick_v[:, h, :], picku[:, h, :])
                    step(m)
                    v.tensor_scalar(half_u[:, 0, :], pick_u, 4, None, ALU.logical_shift_right)
                    step(v.tensor_scalar(half_u[:, 1, :], pick_u, TOPK - 1, None, ALU.bitwise_and))
                    step(v.tensor_copy(half_f, half_u))
                    for s in range(2):
                        step(v.tensor_tensor(eqm, half_f[:, s, :].unsqueeze(2).to_broadcast([P, P, TOPK]),
                                             iota[:, 0:TOPK].unsqueeze(1).to_broadcast([P, P, TOPK]), ALU.is_equal))
                        k = mark(v.tensor_tensor(eqv, eqv, top_i[:, :, s, :].unsqueeze(2).to_broadcast(grid), ALU.mult))
                        split_next()
                        wait_mark(k, hold=False)
                        step(v.tensor_reduce(picks[:, b, s, :], eqm, AX.X, ALU.add))
                    v.tensor_tensor(picks[:, b, 2, :].rearrange("p (h k) -> p h k", h=HEADS), pick_v,
                                    pick_v[:, :, 0:1].to_broadcast(hk), ALU.subtract).then_inc(exp_in, 1)
                    if b == 0:
                        dve.wait_ge(exp_in, 2 * l + 1)
                        dve.sem_inc(dve_held, 1)
                while done[0] < (HALF_ROUNDS - GATE_ROUNDS) * SLOTS + AHEAD:
                    split_next()
                for b in range(TB):
                    gate = picks[:, b, 2, :].rearrange("p (h k) -> p h k", h=HEADS)
                    dve.wait_ge(exp_done, 2 * l + b + 1)
                    step(v.tensor_reduce(gsum[:, 0, :], gate, AX.X, ALU.add))
                    step(v.reciprocal(gsum[:, 1, :], gsum[:, 0, :]))
                    v.tensor_tensor(gate, gate, gsum[:, 1, :].unsqueeze(2).to_broadcast(hk), ALU.mult)\
                        .then_inc(picks_done, 1)
                while done[0] < (HALF_ROUNDS - 1) * SLOTS + AHEAD:
                    split_next()
                for b in range(TB):
                    dve.wait_ge(kt_mm, 2 * l + b + 1)
                    col = slice(b * P, (b + 1) * P)
                    v.tensor_copy(kT[:, 0:3:2, col], ps[:, 6 + b, 0:3 * P].rearrange("p (i t) -> p i t", i=3)[:, 0:3:2, :])
                    v.tensor_scalar(kT[:, 1, col], ps[:, 6 + b, P:2 * P], -1.0, None, ALU.mult).then_inc(kt_done, 1)
                while done[0] < HALF_CHUNKS + AHEAD:
                    split_next()

                acts = big.rearrange("p (n t) -> p n t", t=T)

                def hot(half, n, s):
                    dve.wait_ge(hot_free, l * 2 * HOTS + half * HOTS + n + 1)
                    for t in range(OT):
                        col = bass.ds(n * OT + t, 1)
                        m = v.tensor_scalar(hot1[:, (s % 2) * OT + t, :], iota, kT[:, 0, col], kT[:, 2, col],
                                            ALU.is_equal, ALU.mult)
                    m.then_inc(hot1_ready, 1)

                def gated(half, g, bank):
                    dve.wait_ge(hot_free, 2 + l * 2 * HOTS + half * HOTS + 2 * g + 2)
                    a = acts[:, half * HALF_CHUNKS:(half + 1) * HALF_CHUNKS, bass.ds(g * GT, GT)]
                    v.tensor_tensor(a, a, ps[:, 4 + bank, :].rearrange("p (t n) -> p n t", t=GT), ALU.mult)\
                        .then_inc(g_free, 1)

                def split_w(c, s):
                    dve.wait_ge(whi_ready, l * CHUNKS + c + 1)
                    v.tensor_tensor(w_lo[:, s % AHEAD, :], big[:, bass.ds(c * T, T)], w_hi[:, s % AHEAD, :].bitcast(F32),
                                    ALU.subtract).then_inc(wlo_ready, 1)

                def gate_round(half, i, s, first, last):
                    if not (last and s == SLOTS - 1):
                        hot(half, i * SLOTS + s + 1, (s + 1) % SLOTS)
                    if s == 1 and not first:
                        gated(half, 2 * i - 1, 1)
                    if s == SLOTS - 1:
                        gated(half, 2 * i, 0)

                dve.wait_ge(kt_done, 2 * l + 2)
                hot(0, 0, 0)
                dve.wait_ge(p_free, PBANKS + l * CHUNKS + HALF_CHUNKS)
                dve.sem_inc(dve_held, 1)

                def in_round(i, first=False, last=False):
                    for s in range(SLOTS):
                        gate_round(0, i, s, first, last)
                        split_tile(HALF_CHUNKS + i * SLOTS + s + AHEAD, (s + AHEAD) % SLOTS)

                in_round(0, first=True)
                with dve.Fori(1, HALF_ROUNDS - 1) as i:
                    in_round(i)
                in_round(HALF_ROUNDS - 1, last=True)
                gated(0, GROUPS - 1, 1)

                hot(1, 0, 0)
                for s in range(AHEAD):
                    split_w(s, s)
                dve.wait_ge(p_free, PBANKS + (l + 1) * CHUNKS)
                dve.sem_inc(dve_held, 1)

                def out_round(half, i, first=False, last=False):
                    for s in range(SLOTS):
                        c = half * HALF_CHUNKS + i * SLOTS + s
                        if half == 0:
                            gate_round(1, i, s, first, last)
                        if last and half == 1 and s >= SLOTS - AHEAD:
                            continue
                        split_tile(CHUNKS + c + AHEAD, (s + AHEAD) % SLOTS)
                        if not (last and s >= SLOTS - AHEAD):
                            split_w(c + AHEAD, (s + AHEAD) % SLOTS)

                out_round(0, 0, first=True)
                with dve.Fori(1, HALF_ROUNDS - 1) as i:
                    out_round(0, i)
                out_round(0, HALF_ROUNDS - 1, last=True)
                gated(1, GROUPS - 1, 1)
                for s in range(AHEAD):
                    split_w(HALF_CHUNKS + s, s)
                dve.sem_inc(dve_held, 1)
                with dve.Fori(0, HALF_ROUNDS - 1) as i:
                    out_round(1, i)
                out_round(1, HALF_ROUNDS - 1, last=True)
                dve.wait_ge(tile_mm, (l + 1) * 2 * CHUNKS)
                residual(1, ps_v)
                assert k_step[0] == DVE_STEPS, k_step[0]
            dve.wait_ge(fin_mm, 1)
            v.tensor_scalar(rstd[:], ps[:, 6, 0:T], 1.0 / D, EPS, ALU.mult, ALU.add).then_inc(fin_in, 1)
            dve.wait_ge(fin_root, 1)
            v.reciprocal(rstd[:], rstd[:]).then_inc(dve_step, 1)
            dve.wait_ge(dve_step, LAYERS * DVE_STEPS + 1)
            v.tensor_tensor(h1T, xT[:], rstd[:].unsqueeze(1).to_broadcast([P, KC, T]), ALU.mult)\
                .then_inc(dve_step, 1)
            dve.wait_ge(dve_step, LAYERS * DVE_STEPS + 2)
            for k in range(KC):
                m = v.tensor_scalar(h1T[:, k, :], h1T[:, k, :], final_g[:, k:k + 1], None, ALU.mult)
            m.then_inc(fin_done, 1)


def columns(a):
    a = a.reshape(*a.shape[:-1], -1, P)
    return np.swapaxes(a, -1, -2)


def constants():
    out = np.zeros((P, N_CONST), np.float32)
    out[:, C_ID:C_ID + P] = np.eye(P)
    out[:, C_IOTA:C_IOTA + P] = np.arange(P)
    out[:, C_ONES:C_ONES + P] = 1.0
    d = np.arange(HD)
    angle = 2 * np.pi * (np.outer(d, d) % HD) / HD
    pair = np.eye(2)
    out[:, C_COSD:C_COSD + P] = np.kron(pair, np.cos(angle)) / np.sqrt(HD)
    out[:, C_SIND:C_SIND + P] = -np.kron(pair, np.sin(angle)) / np.sqrt(HD)
    s = np.arange(T)
    angle = 2 * np.pi * (np.outer(s, s) % T) / T
    for at, f in ((C_COSS, np.cos), (C_SINS, np.sin)):
        m = (f(angle) / np.sqrt(T)).reshape(TB, P, T).transpose(1, 0, 2)
        out[:, at:at + TB * T] = m.reshape(P, TB * T)
    return out


def tiles(a):
    l, n = a.shape[:2]
    return a.reshape(l, n // PER_DMA, PER_DMA, P, D).transpose(0, 1, 3, 2, 4).reshape(l, n // PER_DMA, P, PER_DMA * D)


def kernel(**inputs):
    import concourse.bacc as bacc
    from concourse.bass_utils import run_bass_kernel_spmd

    a = {k: np.asarray(v) for k, v in inputs.items()}
    L = LAYERS
    arrays = {}
    arrays["x_in"] = columns(a["x"][0]).transpose(1, 2, 0)
    arrays["c_in"] = columns(a["c"][0])
    arrays["consts_in"] = constants()
    arrays["small_in"] = np.concatenate([
        columns(a["norm1_g"]), columns(a["norm2_g"]),
        columns(np.concatenate([a["gain_a"], a["gain_b"]], -1)),
        a["gmlp_bs"].transpose(0, 2, 1),
        columns(a["mod_b"]),
        a["fnet_w"].reshape(L, PAIRS, P, HD).transpose(0, 2, 1, 3).reshape(L, P, PAIRS * HD),
        a["gmlp_ws"].transpose(0, 3, 1, 2).reshape(L, P, HEADS * P)], -1)
    arrays["fb_in"] = a["fnet_b"].reshape(L, HALF)
    keys = np.stack([a["peer_k1"], a["peer_k2"]], 2)
    arrays["keys_in"] = keys.transpose(0, 4, 1, 2, 3).reshape(L, P, ROWS, KEYS)
    for name, key in (("w_in_in", "w_in"), ("w_out_in", "w_out"), ("wq_in", "peer_wq")):
        w = a[key]
        arrays[name] = w.reshape(L, KC, P, w.shape[-1]).transpose(0, 2, 1, 3)
    arrays["mod_in"] = tiles(a["mod_w"].reshape(L, KC, P, MODS, P).transpose(0, 3, 2, 1, 4).reshape(L, MODS, P, D))
    u = a["peer_u"].reshape(L, KEYS, CHUNKS, KC, P).transpose(0, 2, 4, 3, 1)
    arrays["u_in"] = tiles(u.reshape(L, CHUNKS, P, D))
    arrays["v_in"] = tiles(a["peer_v"].reshape(L, KEYS, CHUNKS, D).transpose(0, 2, 1, 3))
    arrays["final_in"] = columns(a["final_g"])
    arrays = {k: np.ascontiguousarray(v) for k, v in arrays.items()}

    nc = bacc.Bacc("TRN2", target_bir_lowering=False, num_devices=1)
    aps = {k: nc.dram_tensor(k, v.shape, F32, kind="ExternalInput").ap() for k, v in arrays.items()}
    out = nc.dram_tensor("out", (P, KC, T), F32, kind="ExternalOutput").ap()
    build(nc, **aps, out=out)
    r = run_bass_kernel_spmd(nc, [arrays], core_ids=[0])
    y = r.results[0]["out"]
    return np.ascontiguousarray(y.transpose(2, 1, 0).reshape(1, T, D))
```

```python
from contextlib import ExitStack

import numpy as np

import concourse.bass as bass
from concourse import mybir

F32 = mybir.dt.float32
F32R = mybir.dt.float32r
U32 = mybir.dt.uint32
BF16 = mybir.dt.bfloat16
ALU = mybir.AluOpType
ACT = mybir.ActivationFunctionType
AX = mybir.AxisListType

P = 128
D = 1024
T = 256
LAYERS = 2
KC = D // P
TB = T // P
HEADS = 8
HD = 64
WIDTH = HEADS * HD
GC = WIDTH // P
EPS = 1e-6
KEYS = 128
TOPK = 16
ROWS = 2 * HEADS
CHUNKS = KEYS
HALF_CHUNKS = CHUNKS // 2
N_MOD = 6
MODS = N_MOD * KC
NEG = -3.0e38

T_V, T_F, T_U, T_O, T_Q = 0, GC, 2 * GC, 3 * GC, 3 * GC + KC
T_IN = T_Q + ROWS
T_OUT = T_IN + CHUNKS
TILES = T_OUT + CHUNKS
AHEAD = 2
MM_FREE = 2 * AHEAD

SLOTS = 4
RING_FREE = 2 * SLOTS
NEXT = MODS // 2
MOD_ROUNDS = NEXT // SLOTS
HALF_ROUNDS = HALF_CHUNKS // SLOTS
GATE_ROUNDS = 2
PLACES = TILES + MODS
T_LAST = T_OUT + HALF_CHUNKS
assert T_IN % SLOTS == 0 and PLACES % SLOTS == 0 and NEXT % SLOTS == 0
assert T_Q < NEXT < T_IN and NEXT % SLOTS == T_O % SLOTS == T_Q % SLOTS == 0 and 2 * NEXT < HALF_CHUNKS

GT = 8
OT = 4
GROUPS = T // GT
HOTS = T // OT
PBANKS = 4
O_BANKS = (0, 1, 6, 7)

C_COSD, C_SIND, C_ID, C_DFT = 0, P, 2 * P, 3 * P
N_FOURIER = 3 * P + 2 * TB * T
S_NORM1, S_NORM2, S_GAIN, S_BS, S_MODB = 0, 8, 16, 24, 32
S_FW = S_MODB + MODS
S_WS = S_FW + GC * HD
N_SMALL = S_WS + HEADS * P


def place(n):
    if n < NEXT:
        return 2 * n
    if n < T_LAST:
        return n + NEXT
    if n < T_LAST + 2 * NEXT:
        return NEXT + n + (n - T_LAST) // 2
    return n + MODS


def build(nc, x_in, c_in, iota_in, fourier_in, small_in, fb_in, keys_in, w_in_in, w_out_in, wq_in, mod_in, u_in, v_in,
          final_in, g_late, out):
    ctx = ExitStack()
    with ctx:
        def sb(name, shape, dt=F32):
            return ctx.enter_context(nc.sbuf_tensor(name, shape, dt))

        def sem(name):
            return ctx.enter_context(nc.semaphore(name))

        big = sb("expert_acts", [P, CHUNKS * T])
        xT = sb("xT", [P, KC, T])
        h_hi = sb("h_hi", [P, KC, T], F32R)
        h_lo = sb("h_lo", [P, KC, T], F32R)
        ring = sb("ring", [P, SLOTS, D])
        t_hi = sb("tile_hi", [P, AHEAD, D], F32R)
        t_lo = sb("tile_lo", [P, AHEAD, D], F32R)
        w_hi = sb("w_hi", [P, AHEAD, T], F32R)
        w_lo = sb("w_lo", [P, AHEAD, T], F32R)
        iota = sb("iota", [P, P])
        c_row = sb("c_row", [P, D])
        kT = sb("routed", [P, 3, T])
        hot1 = sb("hot1", [P, 2 * OT, P])
        hot2 = sb("hot2", [P, 2 * OT, P])
        stage = sb("g_stage", [P, 2, GT * HD])
        modT = sb("modT", [P, MODS])
        ab = sb("ab", [P, 2, KC])
        final_g = sb("final_g", [P, KC])
        few = sb("few", [P, 4 + SLOTS])
        zero, nothing, eps_ap = few[:, 0:1], few[:, 1:2], few[:, 2:3]
        zeros = few[:, 3:4].bitcast(BF16)[:, 0:1].to_broadcast([P, 512])
        mod_part = few[:, 4:4 + SLOTS]

        at = [0]

        def scratch(n, dt=F32):
            a = big[:, at[0]:at[0] + n]
            at[0] += n
            return a if dt == F32 else a.bitcast(dt)

        fblock = scratch(GC * 256).rearrange("p (r s g e) -> p r s g e", r=GC, s=2, g=2)
        fb_row = scratch(WIDTH)
        uv = scratch(2048).rearrange("p (s b n) -> p s b n", s=2, b=TB)
        zfT = scratch(1024).rearrange("p (r t) -> p r t", r=GC)
        rt = scratch(2048).rearrange("p (b s n) -> p b s n", b=TB, s=2)
        yb = scratch(1024).rearrange("p (b n) -> p b n", b=TB)
        sqv = scratch(1024)
        hA = scratch(KC * T).rearrange("p (k t) -> p k t", k=KC)
        small = scratch(N_SMALL)
        fourier = scratch(N_FOURIER)
        rstd = scratch(T)
        ones = scratch(P)
        stat = scratch(4 * ROWS).rearrange("p (i n) -> p i n", i=4)
        mstat = scratch(16).rearrange("p (i n) -> p i n", i=4)
        assert at[0] <= HALF_CHUNKS * T
        at[0] = HALF_CHUNKS * T
        qT = scratch(ROWS * T).rearrange("p (r t) -> p r t", r=ROWS)
        scores = scratch(TB * ROWS * KEYS).rearrange("p (b r n) -> p b r n", b=TB, r=ROWS)
        keys = scratch(ROWS * KEYS).rearrange("p (r n) -> p r n", r=ROWS)
        left, cand, eq = scratch(2048), scratch(2048), scratch(2048)
        assert at[0] <= CHUNKS * T
        at[0] = HALF_CHUNKS * T
        top_v = scratch(TB * ROWS * TOPK).rearrange("p (b r k) -> p b r k", b=TB, r=ROWS)
        top_iu = scratch(TB * ROWS * TOPK, U32).rearrange("p (b r k) -> p b r k", b=TB, r=ROWS)
        top_i = scratch(TB * ROWS * TOPK).rearrange("p (b h s k) -> p b h s k", b=TB, h=HEADS, s=2)
        pick_v = scratch(P).rearrange("p (h k) -> p h k", h=HEADS)
        pick_u = scratch(P, U32)
        half_u = scratch(2 * P, U32).rearrange("p (s n) -> p s n", s=2)
        half_f = scratch(2 * P).rearrange("p (s n) -> p s n", s=2)
        picks = scratch(TB * 3 * P).rearrange("p (b s n) -> p b s n", b=TB, s=3)
        ident_2 = scratch(P)
        gsum = scratch(2 * HEADS).rearrange("p (s h) -> p s h", s=2)
        assert at[0] <= HALF_CHUNKS * T + ROWS * T

        ident = fourier[:, C_ID:C_ID + P]
        grid = [P, HEADS, TOPK, TOPK]

        def by_rank(a):
            return a.rearrange("p (h k j) -> p h k j", h=HEADS, k=TOPK)

        ps = ctx.enter_context(nc.psum_tensor("ps", [P, 8, 512], F32))

        def half_bank(bank, i):
            return ps[:, bank, i * T:(i + 1) * T]

        once = sem("once_loaded")
        c_ld, silu_done = sem("c_loaded"), sem("silu_done")
        fourier_ld = sem("fourier_loaded")
        small_ld, keys_ld, fb_ld = sem("small_loaded"), sem("keys_loaded"), sem("fb_loaded")
        ring_full = [sem(f"ring_full{q}") for q in range(SLOTS)]
        split_done = sem("split_done")
        hi_ready = sem("hi_ready")
        tile_mm = sem("tile_mm")
        whi_ready, wlo_ready = sem("whi_ready"), sem("wlo_ready")
        x_done = sem("x_done")
        sq_done, sum_mm, root_done = sem("sq_done"), sem("sum_mm"), sem("root_done")
        a_done, hs_in, hs_done = sem("norm_done"), sem("h_hi_done"), sem("h_lo_done")
        fw_mm, fw_done = sem("fw_mm"), sem("fw_done")
        v_done, u_done, zf_done = sem("v_done"), sem("u_done"), sem("zf_done")
        ln_var, ln_root, ln_done = sem("ln_var"), sem("ln_root"), sem("ln_done")
        sv_mm, ya_done = sem("sv_mm"), sem("ya_done")
        rt_mm, rt_done = sem("rt_mm"), sem("rt_done")
        y_mm, yb_done = sem("y_mm"), sem("yb_done")
        ms_done, ms_in, ms_root, yn_done = sem("ms_done"), sem("ms_in"), sem("ms_root"), sem("yn_done")
        tr_mm = sem("tr_mm")
        q_done = sem("q_done")
        s_mm, s_done = sem("s_mm"), sem("s_done")
        exp_in, exp_done = sem("exp_in"), sem("exp_done")
        cand_in, cand_done = sem("cand_in"), sem("cand_done")
        eq_in, eq_done = sem("eq_in"), sem("eq_done")
        picks_done, kt_mm, kt_done = sem("picks_done"), sem("kt_mm"), sem("kt_done")
        p_free = sem("p_free")
        hot1_ready, hot2_ready, hot_free = sem("hot1_ready"), sem("hot2_ready"), sem("hot_free")
        g_free = sem("g_free")
        g_stored = [sem("g_stored0"), sem("g_stored1")]
        g_loaded = [sem("g_loaded0"), sem("g_loaded1")]
        stage_free = sem("stage_free")
        g_late_used = sem("g_late_used")
        act_step = sem("act_step")
        dve_norm = sem("dve_norm")
        mod_step = sem("mod_step")
        dve_step = sem("dve_step")
        zeros_done = sem("zeros_done")
        ones_done = sem("ones_done")
        dve_held, pe_held, sp_held = sem("dve_held"), sem("pe_held"), sem("sp_held")
        fin_root, fin_done = sem("fin_root"), sem("fin_done")
        out_st = sem("out_stored")
        DVE_STEPS = 173

        def products(l, n):
            return MM_FREE + l * 2 * TILES + 2 * n + 2

        def splits(l, at_, h):
            return RING_FREE + 2 * NEXT + l * 2 * PLACES + 2 * at_ + h + 1

        def full(l, at_, s):
            return (NEXT + l * PLACES + at_) * (16 // SLOTS) + (16 - 16 // SLOTS * s)

        block = ctx.enter_context(nc.Block())

        @block.sync
        def _(sp):
            def fetch(place_, s, src, l, n, hold=False):
                sp.wait_ge(split_done, 2 * place_ + 2)
                if hold:
                    sp.sem_inc(sp_held, 1)
                sp.dma_start(ring[:, s, :], src[bass.ds(l, 1), bass.ds(n, 1)].rearrange("a b p n -> (a b p) n"))\
                    .then_inc(ring_full[s], 16)

            def fetch_all(start, src, l, tiles_):
                with sp.Fori(0, tiles_ // SLOTS) as r:
                    for s in range(SLOTS):
                        fetch(start + r * SLOTS + s, s, src, l, r * SLOTS + s)

            with sp.Fori(0, MOD_ROUNDS) as r:
                for s in range(SLOTS):
                    fetch(r * SLOTS + s, s, mod_in, 0, r * SLOTS + s)
            with sp.Fori(0, LAYERS) as l:
                base = NEXT + l * PLACES

                def fetch_with_mods(first, src, tiles_):
                    with sp.Fori(0, tiles_ // SLOTS) as r:
                        for s in range(SLOTS):
                            start = base + 2 * first + r * 2 * SLOTS + 2 * s
                            fetch(start, 2 * s % SLOTS, src, l, r * SLOTS + s)
                            fetch(start + 1, (2 * s + 1) % SLOTS, mod_in, l, r * SLOTS + NEXT + first + s)

                fetch_with_mods(0, w_in_in, T_O)
                fetch_with_mods(T_O, w_out_in, KC)
                fetch_with_mods(T_Q, wq_in, NEXT - T_Q)
                with sp.Fori((NEXT - T_Q) // SLOTS, ROWS // SLOTS) as r:
                    for s in range(SLOTS):
                        fetch(base + T_Q + NEXT + r * SLOTS + s, s, wq_in, l, r * SLOTS + s)
                fetch_all(base + T_IN + NEXT, u_in, l, CHUNKS)
                fetch_all(base + T_OUT + NEXT, v_in, l, HALF_CHUNKS)
                with sp.Fori(0, MOD_ROUNDS) as r:
                    for s in range(2 * SLOTS):
                        start = base + T_LAST + NEXT + r * 3 * SLOTS + s + s // 2
                        fetch(start, (s + s // 2) % SLOTS, v_in, l, r * 2 * SLOTS + HALF_CHUNKS + s)
                        if s % 2:
                            fetch(start + 1, (s + s // 2 + 1) % SLOTS, mod_in, (LAYERS - 1) - l, r * SLOTS + s // 2,
                                  hold=True)
                with sp.Fori(2 * MOD_ROUNDS, HALF_ROUNDS) as r:
                    for s in range(SLOTS):
                        fetch(base + T_LAST + MODS + r * SLOTS + s, s, v_in, l, r * SLOTS + HALF_CHUNKS + s)
            sp.wait_ge(fin_done, 1)
            sp.dma_start(out, hA).then_inc(out_st, 16)
            sp.wait_ge(out_st, 16)

        @block.gpsimd
        def _(pool):
            pool.dma_start(c_row[:], c_in.to_broadcast([P, D])).then_inc(c_ld, 16)
            pool.dma_start(xT[:], x_in).then_inc(once, 16)
            pool.dma_start(iota[:], iota_in).then_inc(once, 16)
            pool.dma_start(final_g[:], final_in).then_inc(once, 16)
            with pool.Fori(0, LAYERS) as l:
                pool.wait_ge(g_late_used, 2 + l * GROUPS)
                pool.dma_start(small, small_in[bass.ds(l, 1)].rearrange("a p n -> (a p) n")).then_inc(small_ld, 16)
                pool.dma_start(fourier, fourier_in).then_inc(fourier_ld, 16)
                pool.dma_start(fb_row, fb_in[bass.ds(l, 1)].to_broadcast([P, WIDTH])).then_inc(fb_ld, 16)
                pool.wait_ge(x_done, KC + l * 2 * KC)
                pool.dma_start(keys, keys_in[bass.ds(l, 1)].rearrange("a p k n -> (a p) k n")).then_inc(keys_ld, 16)
                def sums(b):
                    pool.wait_ge(cand_in, 2 * l + b + 1)
                    vals = top_v[:, b].rearrange("p (h s) k -> p h s k", s=2)
                    nc.gpsimd.tensor_tensor(by_rank(cand), vals[:, :, 0, :].unsqueeze(3).to_broadcast(grid),
                                            vals[:, :, 1, :].unsqueeze(2).to_broadcast(grid), ALU.add).then_inc(cand_done, 1)

                def places(b):
                    for i, buf in enumerate((eq, left)):
                        pool.wait_ge(eq_in, 4 * l + 2 * b + i + 1)
                        nc.gpsimd.tensor_tensor(by_rank(buf), by_rank(buf), top_i[:, b, :, i, :].unsqueeze(2).to_broadcast(grid),
                                                ALU.mult).then_inc(eq_done, 1)

                sums(0)
                sums(1)
                places(0)
                places(1)
                with pool.Fori(0, GROUPS // 2) as r:
                    for q in range(2):
                        pool.wait_ge(g_free, 2 + l * GROUPS + r * 2 + q + 1)
                        pool.dma_start(g_late[bass.ds(r * 2 + q, 1)].rearrange("a p n -> (a p) n"), stage[:, q, :])\
                            .then_inc(g_stored[q], 16)
                        pool.wait_ge(g_stored[q], l * 8 * GROUPS + r * 16 + 16)
                        pool.sem_inc(stage_free, 1)
                with pool.Fori(0, GROUPS // 2) as r:
                    for q in range(2):
                        pool.wait_ge(g_late_used, l * GROUPS + r * 2 + q + 1)
                        pool.dma_start(stage[:, q, :], g_late[bass.ds(r * 2 + q, 1)].rearrange("a p n -> (a p) n"))\
                            .then_inc(g_loaded[q], 16)

        @block.tensor
        def _(pe):
            def mm(out, lhsT, rhs, start, stop):
                return nc.tensor.matmul(out, lhsT, rhs, start=start, stop=stop, skip_group_check=True)

            def split_mm(out, a, b, start, stop):
                mm(out, a[0], b[0], start, False)
                mm(out, a[0], b[1], False, False)
                return mm(out, a[1], b[0], False, stop)

            def tile(s, i):
                return t_hi[:, s, i * P:(i + 1) * P], t_lo[:, s, i * P:(i + 1) * P]

            def h(k, cols=slice(0, T)):
                return h_hi[:, k, cols], h_lo[:, k, cols]

            pe.sem_inc(tile_mm, MM_FREE)
            pe.wait_ge(once, 48)
            pe.wait_ge(zeros_done, 1)
            with pe.Fori(0, LAYERS) as l:
                def column_sums(n, bank):
                    for k in range(KC):
                        pe.wait_ge(sq_done, l * 2 * KC + n * KC + k + 1)
                        m = mm(half_bank(bank, 0), ones, hA[:, k, :], k == 0, k == KC - 1)
                    m.then_inc(sum_mm, 1)

                def wait_h(n, k):
                    pe.wait_ge(hs_done, (l * 3 + n) * KC + k + 1)

                pe.wait_ge(ones_done, l + 1)
                column_sums(0, 6)
                pe.wait_ge(small_ld, 16 * l + 16)
                pe.wait_ge(fourier_ld, 16 * l + 16)
                mm(ps[:, 7, 0:256], fourier[:, C_COSD:C_COSD + P], small[:, S_FW:S_FW + 256], True, True)
                mm(ps[:, 7, 256:512], fourier[:, C_SIND:C_SIND + P], small[:, S_FW:S_FW + 256], True, True)\
                    .then_inc(fw_mm, 1)

                def by_token(first, j, banks):
                    n = first + j
                    for i in range(2):
                        pe.wait_ge(split_done, splits(l, place(n), i))
                        k = 2 * j + i
                        if first == 0:
                            wait_h(0, k)
                        w = slice(i * WIDTH, (i + 1) * WIDTH)
                        for b in range(TB):
                            m = split_mm(ps[:, banks[b], :], h(k, slice(b * P, (b + 1) * P)),
                                         (t_hi[:, n % AHEAD, w], t_lo[:, n % AHEAD, w]), k == 0, k == KC - 1)
                        m.then_inc(tile_mm, 1)

                def by_column(n, out, first=None):
                    for i in range(2):
                        pe.wait_ge(split_done, splits(l, place(n), i))
                        for k in range(4 * i, 4 * i + 4):
                            if first is not None:
                                wait_h(first, k)
                            m = split_mm(out, tile(n % AHEAD, k), h(k), k == 0, k == KC - 1)
                        m.then_inc(tile_mm, 1)

                for c in range(GC):
                    by_token(T_V, c, (0, 1))
                for c in range(GC):
                    by_column(T_F + c, half_bank(4 + c // 2, c % 2))
                pe.wait_ge(fw_done, l + 1)
                by_token(T_U, 0, (6, 7))
                pe.wait_ge(zf_done, 2 * l + 2)
                for b in range(TB):
                    for r in range(GC):
                        m = mm(half_bank(2 + 2 * b + r // 2, r % 2), zfT[:, r, b * P:(b + 1) * P],
                               fblock[:, r].rearrange("p s g e -> p (s g e)"), True, True)
                    m.then_inc(rt_mm, 1)
                for c in range(1, GC):
                    by_token(T_U, c, (6, 7))
                pe.wait_ge(ln_done, l + 1)
                for g in range(HEADS):
                    m = mm(ps[:, g // 4, (g % 4) * P:(g % 4 + 1) * P], small[:, S_WS + g * P:S_WS + (g + 1) * P],
                           uv[:, 1, :, g * HD:(g + 1) * HD], True, True)
                m.then_inc(sv_mm, 1)
                pe.wait_ge(rt_done, 2 * l + 2)
                for tp in range(TB):
                    n = 0
                    for b in range(TB):
                        for s in range(2):
                            o = C_DFT + (s * TB + b) * T + tp * P
                            m = mm(ps[:, 2 + tp, :], fourier[:, o:o + P], rt[:, b, s, :], n == 0, n == 2 * TB - 1)
                            n += 1
                    m.then_inc(y_mm, 1)

                def transposed(g, y, bank):
                    pe.wait_ge(yn_done, 2 * l + g + 1)
                    for c in range(GC):
                        for b in range(TB):
                            m = nc.tensor.transpose(ps[:, bank + c // 2, (c % 2) * T + b * P:(c % 2) * T + (b + 1) * P],
                                                    y[:, b, c * P:(c + 1) * P], ident)
                    m.then_inc(tr_mm, 1)

                def project(g):
                    for j in range(GC):
                        n = T_O + g * GC + j
                        for i in range(2):
                            pe.wait_ge(split_done, splits(l, place(n), i))
                            for c in range(GC):
                                if j == 0 and i == 0:
                                    wait_h(1, g * GC + c)
                                m = split_mm(half_bank(O_BANKS[j], i), tile(n % AHEAD, 4 * i + c), h(g * GC + c),
                                             False, False)
                            m.then_inc(tile_mm, 1)

                transposed(0, uv[:, 0], 4)
                for bank in O_BANKS:
                    mm(ps[:, bank, :], iota[:, 0:P // 2].bitcast(BF16), zeros, True, False)
                project(0)
                transposed(1, yb, 2)
                project(1)
                column_sums(1, 2)
                for r in range(ROWS):
                    by_column(T_Q + r, half_bank(r // 2, r % 2), 2 if r == 0 else None)
                pe.wait_ge(keys_ld, 16 * l + 16)
                for b in range(TB):
                    pe.wait_ge(q_done, (l + 1) * (ROWS // 2))
                    for r in range(ROWS):
                        m = mm(ps[:, 4 - 4 * b + r // 4, (r % 4) * P:(r % 4 + 1) * P], qT[:, r, b * P:(b + 1) * P],
                               keys[:, r, :], True, True)
                    m.then_inc(s_mm, 1)

                def expert_in(c, at_, s):
                    pe.wait_ge(p_free, l * CHUNKS + c + 1)
                    for i in range(2):
                        pe.wait_ge(split_done, splits(l, at_, i))
                        for k in range(4 * i, 4 * i + 4):
                            m = split_mm(half_bank(s % PBANKS, 0), tile(s % AHEAD, k), h(k), k == 0, k == KC - 1)
                        m.then_inc(tile_mm, 1)

                def expert_out(c, at_, s):
                    pe.wait_ge(wlo_ready, l * CHUNKS + c + 1)
                    for i in range(2):
                        pe.wait_ge(split_done, splits(l, at_, i))
                        for d in range(4 * i, 4 * i + 4):
                            m = split_mm(half_bank(d // 2, d % 2), tile(s % AHEAD, d),
                                         (w_hi[:, s % AHEAD, :], w_lo[:, s % AHEAD, :]), False, False)
                        m.then_inc(tile_mm, 1)

                def scatter(i, s):
                    n = i * SLOTS + s
                    pe.wait_ge(hot1_ready, l * HOTS + n + 1)
                    pe.wait_ge(hot2_ready, l * HOTS + n + 1)
                    if s % 2 == 0:
                        pe.wait_ge(g_free, l * GROUPS + i * 2 + s // 2 + 1)
                    for t in range(OT):
                        o = (s % 2) * OT + t
                        m = mm(ps[:, 4 + s, t * P:(t + 1) * P], hot1[:, o, :], hot2[:, o, :], True, True)
                    m.then_inc(hot_free, 1)

                pe.wait_ge(s_done, 2 * l + 2)
                pe.sem_inc(pe_held, 1)
                with pe.Fori(0, HALF_ROUNDS - 1) as r:
                    for s in range(SLOTS):
                        expert_in(r * SLOTS + s, r * SLOTS + T_IN + NEXT + s, s)
                for b in range(TB):
                    pe.wait_ge(picks_done, 2 * l + b + 1)
                    for i in range(3):
                        m = nc.tensor.transpose(ps[:, 6 + b, i * P:(i + 1) * P], picks[:, b, i, :], ident_2)
                    m.then_inc(kt_mm, 1)
                for s in range(SLOTS):
                    c = (HALF_ROUNDS - 1) * SLOTS + s
                    expert_in(c, T_IN + NEXT + c, s)
                with pe.Fori(0, HALF_ROUNDS) as i:
                    for s in range(SLOTS):
                        expert_in(i * SLOTS + HALF_CHUNKS + s, i * SLOTS + T_IN + HALF_CHUNKS + NEXT + s, s)
                        scatter(i, s)
                pe.wait_ge(p_free, PBANKS + (l + 1) * CHUNKS)
                for b in range(4):
                    mm(ps[:, b, :], iota[:, 0:P // 2].bitcast(BF16), zeros, True, False)
                with pe.Fori(0, HALF_ROUNDS) as i:
                    for s in range(SLOTS):
                        expert_out(i * SLOTS + s, i * SLOTS + T_OUT + NEXT + s, s)
                with pe.Fori(0, MOD_ROUNDS) as i:
                    for s in range(2 * SLOTS):
                        expert_out(i * 2 * SLOTS + HALF_CHUNKS + s, i * 3 * SLOTS + T_LAST + NEXT + s + s // 2, s)
                with pe.Fori(2 * MOD_ROUNDS, HALF_ROUNDS) as i:
                    for s in range(SLOTS):
                        expert_out(i * SLOTS + HALF_CHUNKS + s, i * SLOTS + T_LAST + MODS + s, s)
            pe.wait_ge(ones_done, LAYERS + 1)
            for k in range(KC):
                pe.wait_ge(sq_done, LAYERS * 2 * KC + k + 1)
                m = mm(half_bank(6, 0), ones, hA[:, k, :], k == 0, k == KC - 1)
            m.then_inc(sum_mm, 1)

        @block.scalar
        def _(act):
            A = nc.scalar.activation

            act.wait_ge(zeros_done, 1)
            act.wait_ge(c_ld, 16)
            A(c_row[:], c_row[:], ACT.Silu).then_inc(silu_done, 1)
            with act.Fori(0, LAYERS) as l:
                def split(n, at_, s):
                    for i in range(2):
                        act.wait_ge(tile_mm, l * 2 * TILES + 2 * n + i + 1)
                        if i == 0:
                            act.wait_ge(ring_full[s % SLOTS], full(l, at_, s % SLOTS))
                        col = slice(i * D // 2, (i + 1) * D // 2)
                        A(t_hi[:, split_slot(n, s), col], ring[:, s % SLOTS, col], ACT.Copy).then_inc(hi_ready, 1)

                def split_slot(n, s):
                    return n % AHEAD if isinstance(n, int) else parity[0]

                parity = [0]

                def S(n):
                    split(n, place(n), place(n) % SLOTS)

                def squares(n):
                    for k in range(KC):
                        act.wait_ge(x_done, l * 2 * KC + n * KC + k + 1)
                        A(hA[:, k, :], xT[:, k, :], ACT.Square).then_inc(sq_done, 1)

                def keep(f):
                    A(nothing, zero, f)

                def root(n, bank):
                    keep(ACT.Sqrt)
                    act.wait_ge(sum_mm, 2 * l + n + 1)
                    A(rstd, half_bank(bank, 0), ACT.Sqrt, bias=eps_ap, scale=1.0 / D).then_inc(root_done, 1)

                def shifted(n):
                    for k in range(KC):
                        act.wait_ge(a_done, l * 2 * KC + n * KC + k + 1)
                        A(h_hi[:, k, :], hA[:, k, :], ACT.Identity, bias=modT[:, 3 * KC * n + k:3 * KC * n + k + 1])\
                            .then_inc(hs_in, 1)

                squares(0)
                S(0)
                S(1)
                root(0, 6)
                shifted(0)
                for n in range(2, 6):
                    S(n)
                for b in range(TB):
                    act.wait_ge(tile_mm, products(l, T_V + GC - 1))
                    m = A(uv[:, 1, b, :], ps[:, b, :], ACT.Gelu)
                m.then_inc(v_done, 1)
                S(6)
                S(7)
                act.wait_ge(tile_mm, products(l, T_F + 1))
                A(zfT[:, 0:2, :], ps[:, 4, :].rearrange("p (r t) -> p r t", r=2), ACT.Copy).then_inc(zf_done, 1)
                keep(ACT.Sqrt)
                act.wait_ge(ln_var, l + 1)
                A(stat[:, 3, :], stat[:, 2, :], ACT.Sqrt).then_inc(ln_root, 1)
                S(8)
                S(9)
                act.wait_ge(tile_mm, products(l, T_F + 3))
                A(zfT[:, 2:4, :], ps[:, 5, :].rearrange("p (r t) -> p r t", r=2), ACT.Copy).then_inc(zf_done, 1)
                S(10)
                for b in range(TB):
                    act.wait_ge(rt_mm, 2 * l + b + 1)
                    src = ps[:, 2 + 2 * b:4 + 2 * b, :].rearrange("p c (r s n) -> p (c r) s n", r=2, s=2)
                    A(rt[:, b].rearrange("p s (r n) -> p r s n", r=GC), src, ACT.Copy).then_inc(rt_done, 1)
                S(11)
                S(12)
                for b in range(TB):
                    act.wait_ge(tile_mm, products(l, T_U + GC - 1))
                    m = A(uv[:, 0, b, :], ps[:, 6 + b, :], ACT.Gelu)
                m.then_inc(u_done, 1)
                S(13)

                def mean_squares(g, y):
                    for b in range(TB):
                        m = A(hA[:, 2 * (2 * g + b):2 * (2 * g + b) + 2, :].rearrange("p k t -> p (k t)"), y[:, b, :],
                              ACT.Square, accum_out=mstat[:, 0, 2 * g + b:2 * g + b + 1])
                    m.then_inc(ms_done, 1)
                    keep(ACT.Sqrt)
                    act.wait_ge(ms_in, 2 * l + g + 1)
                    A(mstat[:, 2, 2 * g:2 * g + 2], mstat[:, 1, 2 * g:2 * g + 2], ACT.Sqrt).then_inc(ms_root, 1)

                def gained(g, bank):
                    act.wait_ge(tr_mm, 2 * l + g + 1)
                    for c in range(GC):
                        k = g * GC + c
                        A(h_hi[:, k, :], half_bank(bank + c // 2, c % 2), ACT.Copy,
                          scale=small[:, S_GAIN + k:S_GAIN + k + 1]).then_inc(hs_in, 1)

                act.wait_ge(ya_done, l + 1)
                mean_squares(0, uv[:, 0])
                gained(0, 4)
                act.wait_ge(yb_done, l + 1)
                mean_squares(1, yb)
                for n in range(14, 18):
                    S(n)
                gained(1, 2)
                for j in range(GC):
                    S(18 + j)
                    for k in (2 * j, 2 * j + 1):
                        act.wait_ge(x_done, l * 2 * KC + KC + k + 1)
                        A(hA[:, k, :], xT[:, k, :], ACT.Square).then_inc(sq_done, 1)
                root(1, 2)
                shifted(1)
                for r in range(ROWS):
                    if r % 2:
                        act.wait_ge(tile_mm, products(l, T_Q + r))
                        A(qT[:, r - 1:r + 1, :], ps[:, r // 2, :].rearrange("p (r t) -> p r t", r=2), ACT.Copy)\
                            .then_inc(q_done, 1)
                    S(T_Q + r + AHEAD)
                act.wait_ge(s_mm, 2 * l + 1)
                A(scores[:, 0], ps[:, 4:8, :].rearrange("p c (r n) -> p (c r) n", r=4), ACT.Copy).then_inc(s_done, 1)

                def next_tile(c, half, places, s):
                    parity[0] = s % AHEAD
                    split(c + (T_IN, T_OUT)[half] + AHEAD, places, s + AHEAD)

                def gelu(c, s):
                    act.wait_ge(tile_mm, products(l, c + T_IN))
                    A(big[:, bass.ds(c * T, T)], half_bank(s % PBANKS, 0), ACT.Gelu).then_inc(p_free, 1)

                def split_w(c, s):
                    A(w_hi[:, s % AHEAD, :], big[:, bass.ds(c * T, T)], ACT.Copy).then_inc(whi_ready, 1)

                def hot(n, s):
                    o = (s % 2) * OT
                    act.wait_ge(hot_free, l * HOTS + n + 1)
                    for t in range(OT):
                        m = A(hot2[:, o + t, :], iota[:], ACT.Abs,
                              bias=kT[:, 1, bass.ds(n * OT + t, 1)])
                    m.then_inc(act_step, 1)
                    act.wait_ge(act_step, l * HOTS + n + 1)
                    A(hot2[:, o:o + OT, :], hot2[:, o:o + OT, :], ACT.Relu, bias=1.0, scale=-1.0).then_inc(hot2_ready, 1)

                def first_half(r0, r1):
                    with act.Fori(r0, r1) as r:
                        keep(ACT.Gelu)
                        for s in range(SLOTS):
                            gelu_then_split(r * SLOTS + s, s)

                def gelu_then_split(c, s):
                    next_tile(c, 0, c + T_IN + NEXT + AHEAD, s)
                    gelu(c, s)

                first_half(0, HALF_ROUNDS - GATE_ROUNDS)
                for b in range(TB):
                    act.wait_ge(exp_in, 2 * l + b + 1)
                    g = picks[:, b, 2, :]
                    A(g, g, ACT.Exp).then_inc(exp_done, 1)
                first_half(HALF_ROUNDS - GATE_ROUNDS, HALF_ROUNDS)

                act.wait_ge(kt_done, 2 * l + 2)
                hot(0, 0)

                def in_round(i, last):
                    keep(ACT.Gelu)
                    for s in range(SLOTS):
                        c = i * SLOTS + HALF_CHUNKS + s
                        next_tile(c, 0, c + T_IN + NEXT + AHEAD, s)
                        gelu(c, s)
                        if not (last and s == SLOTS - 1):
                            hot(i * SLOTS + s + 1, (s + 1) % SLOTS)

                with act.Fori(0, HALF_ROUNDS - 1) as i:
                    in_round(i, False)
                in_round(HALF_ROUNDS - 1, True)

                act.wait_ge(g_free, 2 + (l + 1) * GROUPS)
                for s in range(AHEAD):
                    split_w(s, s)

                def out_round(i, last):
                    for s in range(SLOTS):
                        c = i * SLOTS + s
                        if last:
                            S(T_OUT + c + AHEAD)
                        else:
                            next_tile(c, 1, c + T_OUT + NEXT + AHEAD, s)
                        if not (last and s >= SLOTS - AHEAD):
                            split_w(c + AHEAD, (s + AHEAD) % SLOTS)

                with act.Fori(0, HALF_ROUNDS - 1) as i:
                    out_round(i, False)
                out_round(HALF_ROUNDS - 1, True)
                act.wait_ge(g_late_used, 2 + (l + 1) * GROUPS)
                for s in range(AHEAD):
                    act.wait_ge(tile_mm, products(l, T_LAST - AHEAD + s))
                    split_w(HALF_CHUNKS + s, s)

                def mod_round(i, last):
                    for s in range(2 * SLOTS):
                        c = i * 2 * SLOTS + HALF_CHUNKS + s
                        if last:
                            S(T_OUT + c + AHEAD)
                        else:
                            parity[0] = s % AHEAD
                            j = s + AHEAD
                            split(c + T_OUT + AHEAD, i * 3 * SLOTS + T_LAST + NEXT + j + j // 2, (j + j // 2) % SLOTS)
                        split_w(c + AHEAD, s)

                with act.Fori(0, MOD_ROUNDS - 1) as i:
                    mod_round(i, False)
                mod_round(MOD_ROUNDS - 1, True)
                with act.Fori(2 * MOD_ROUNDS, HALF_ROUNDS - 1) as i:
                    for s in range(SLOTS):
                        c = i * SLOTS + HALF_CHUNKS + s
                        next_tile(c, 1, c + T_OUT + MODS + AHEAD, s)
                        split_w(c + AHEAD, s)
                for s in range(SLOTS - AHEAD):
                    c = CHUNKS - SLOTS + s
                    S(T_OUT + c + AHEAD)
                    split_w(c + AHEAD, s)
            for k in range(KC):
                act.wait_ge(x_done, LAYERS * 2 * KC + k + 1)
                A(hA[:, k, :], xT[:, k, :], ACT.Square).then_inc(sq_done, 1)
            A(nothing, zero, ACT.Sqrt)
            act.wait_ge(sum_mm, 2 * LAYERS + 1)
            A(rstd, half_bank(6, 0), ACT.Sqrt, bias=eps_ap, scale=1.0 / D).then_inc(fin_root, 1)

        @block.vector
        def _(dve):
            v = nc.vector
            v.memset(few[:, 0:2], 0.0)
            v.memset(few[:, 3:4], 0.0)
            v.memset(eps_ap, EPS).then_inc(zeros_done, 1)
            dve.sem_inc(split_done, RING_FREE)
            dve.sem_inc(hot_free, 2)
            dve.sem_inc(g_free, 2)
            dve.sem_inc(g_late_used, 2)
            dve.sem_inc(stage_free, 2)
            dve.sem_inc(p_free, PBANKS)

            def mod_tile(at_full, slot, total):
                dve.wait_ge(ring_full[slot], at_full)
                dve.sem_inc(dve_held, 1)
                return v.tensor_tensor_reduce(out=ring[:, slot, :], in0=ring[:, slot, :], in1=c_row[:], op0=ALU.mult,
                                              op1=ALU.add, scale=1.0, scalar=0.0,
                                              accum_out=total).then_inc(split_done, 2)

            def keep_mods(r):
                dve.sem_inc(dve_held, 1)
                v.tensor_copy(modT[:, bass.ds(r * SLOTS, SLOTS)], mod_part).then_inc(mod_step, 1)

            dve.wait_ge(silu_done, 1)
            with dve.Fori(0, MOD_ROUNDS) as r:
                for s in range(SLOTS):
                    mod_tile(16 * r + 16, s, mod_part[:, s:s + 1])
                dve.wait_ge(split_done, RING_FREE + 2 * SLOTS * r + 2 * SLOTS)
                keep_mods(r)
                dve.wait_ge(mod_step, r + 1)
            dve.wait_ge(once, 48)
            dve.sem_inc(x_done, KC)

            def norm(l, n):
                dve.wait_ge(root_done, 2 * l + n + 1)
                v.reciprocal(rstd, rstd).then_inc(dve_norm, 1)
                dve.wait_ge(dve_norm, 2 * l + n + 1)
                for k in range(KC + 1):
                    if k < KC:
                        v.scalar_tensor_tensor(out=hA[:, k, :], in0=xT[:, k, :], scalar=ab[:, n, k:k + 1], in1=rstd,
                                               op0=ALU.mult, op1=ALU.mult).then_inc(a_done, 1)
                    if k > 0:
                        j = k - 1
                        dve.wait_ge(hs_in, (l * 3 + 2 * n) * KC + j + 1)
                        at_ = 3 * KC * n + j
                        v.scalar_tensor_tensor(out=h_lo[:, j, :], in0=hA[:, j, :], scalar=modT[:, at_:at_ + 1],
                                               in1=h_hi[:, j, :].bitcast(F32), op0=ALU.add, op1=ALU.subtract)\
                            .then_inc(hs_done, 1)

            with dve.Fori(0, LAYERS) as l:
                k_step = [0]

                def step(m, hold=False):
                    k_step[0] += 1
                    m.then_inc(dve_step, 1)
                    dve.wait_ge(dve_step, l * DVE_STEPS + k_step[0])
                    if hold:
                        dve.sem_inc(dve_held, 1)

                def mark(m):
                    k_step[0] += 1
                    m.then_inc(dve_step, 1)
                    return k_step[0]

                def wait_mark(k, hold=True):
                    dve.wait_ge(dve_step, l * DVE_STEPS + k)
                    if hold:
                        dve.sem_inc(dve_held, 1)

                def split(n, slot, s):
                    for i in range(2):
                        dve.wait_ge(hi_ready, l * 2 * TILES + 2 * n + i + 1)
                        col = slice(i * D // 2, (i + 1) * D // 2)
                        v.tensor_tensor(t_lo[:, s % AHEAD, col], ring[:, slot, col], t_hi[:, s % AHEAD, col].bitcast(F32),
                                        ALU.subtract).then_inc(split_done, 1)

                def S(n):
                    split(n, place(n) % SLOTS, n)

                def second_mod(n):
                    at_ = place(n) + 1
                    mod_tile(full(l, at_, at_ % SLOTS), at_ % SLOTS, modT[:, NEXT + n:NEXT + n + 1])

                v.memset(ones, 1.0).then_inc(ones_done, 1)
                fblock_cleared = mark(v.memset(fblock, 0.0))
                dve.wait_ge(x_done, KC + l * 2 * KC)
                dve.wait_ge(small_ld, 16 * l + 16)

                def add_bias(first, n):
                    cols = slice(first, first + n)
                    step(v.tensor_tensor(modT[:, cols], modT[:, cols], small[:, S_MODB + first:S_MODB + first + n], ALU.add))

                def scales(n, at_):
                    first = (3 * n + 1) * KC
                    step(v.scalar_tensor_tensor(out=ab[:, n, :], in0=modT[:, first:first + KC], scalar=1.0,
                                                in1=small[:, at_:at_ + KC], op0=ALU.add, op1=ALU.mult))

                add_bias(0, NEXT)
                scales(0, S_NORM1)
                S(0)
                second_mod(0)
                S(1)
                norm(l, 0)
                second_mod(1)
                dve.wait_ge(fw_mm, l + 1)
                wait_mark(fblock_cleared)
                for g in range(2):
                    half = slice(g * HD, (g + 1) * HD)
                    for s in range(2):
                        m = v.tensor_copy(fblock[half, :, s, g, :],
                                          ps[half, 7, s * 256:(s + 1) * 256].rearrange("p (r e) -> p r e", r=GC))
                m.then_inc(fw_done, 1)
                for n in range(2, 6):
                    S(n)
                    second_mod(n)
                dve.wait_ge(v_done, l + 1)
                vh = uv[:, 1].rearrange("p b (h d) -> p b h d", h=HEADS)
                sqh = sqv.rearrange("p (b h d) -> p b h d", b=TB, h=HEADS)

                def st(i):
                    return stat[:, i, :].rearrange("p (b h) -> p b h", b=TB)

                def wide(i):
                    return st(i).unsqueeze(3).to_broadcast([P, TB, HEADS, HD])

                step(v.tensor_reduce(st(0), vh, AX.X, ALU.add))
                k = mark(v.tensor_scalar(stat[:, 1, :], stat[:, 0, :], -1.0 / HD, None, ALU.mult))
                S(6)
                wait_mark(k, hold=False)
                k = mark(v.tensor_tensor(vh, vh, wide(1), ALU.add))
                second_mod(6)
                wait_mark(k, hold=False)
                k = mark(v.tensor_tensor(sqh, vh, vh, ALU.mult))
                S(7)
                wait_mark(k, hold=False)
                step(v.tensor_reduce(st(0), sqh, AX.X, ALU.add))
                v.tensor_scalar(stat[:, 2, :], stat[:, 0, :], 1.0 / HD, EPS, ALU.mult, ALU.add).then_inc(ln_var, 1)
                second_mod(7)
                dve.wait_ge(ln_root, l + 1)
                step(v.reciprocal(stat[:, 1, :], stat[:, 3, :]))
                v.tensor_tensor(vh, vh, wide(1), ALU.mult).then_inc(ln_done, 1)
                for n in range(8, T_O + AHEAD):
                    S(n)
                    second_mod(n)
                dve.wait_ge(sv_mm, l + 1)
                dve.wait_ge(u_done, l + 1)
                for h in range(HEADS):
                    u = uv[:, 0, :, h * HD:(h + 1) * HD]
                    m = v.scalar_tensor_tensor(out=u, in0=ps[:, h // 4, (h % 4) * P:(h % 4 + 1) * P].rearrange(
                        "p (b d) -> p b d", b=TB), scalar=small[:, S_BS + h:S_BS + h + 1], in1=u, op0=ALU.add, op1=ALU.mult)
                m.then_inc(ya_done, 1)

                def normalised(g, y):
                    sl = slice(2 * g, 2 * g + 2)
                    dve.wait_ge(ms_done, 2 * l + g + 1)
                    v.tensor_scalar(mstat[:, 1, sl], mstat[:, 0, sl], 1.0 / WIDTH, EPS, ALU.mult, ALU.add)\
                        .then_inc(ms_in, 1)
                    dve.wait_ge(ms_root, 2 * l + g + 1)
                    step(v.reciprocal(mstat[:, 3, sl], mstat[:, 2, sl]))
                    for b in range(TB):
                        m = v.tensor_scalar(y[:, b, :], y[:, b, :], mstat[:, 3, 2 * g + b:2 * g + b + 1], None, ALU.mult)
                    m.then_inc(yn_done, 1)

                def gained(g, bank):
                    for c in range(GC):
                        k = g * GC + c
                        if c % 2 == 0:
                            dve.wait_ge(hs_in, (l * 3 + 1) * KC + k + 2)
                        v.scalar_tensor_tensor(out=h_lo[:, k, :], in0=half_bank(bank + c // 2, c % 2),
                                               scalar=small[:, S_GAIN + k:S_GAIN + k + 1], in1=h_hi[:, k, :].bitcast(F32),
                                               op0=ALU.mult, op1=ALU.subtract).then_inc(hs_done, 1)

                normalised(0, uv[:, 0])
                dve.wait_ge(fb_ld, 16 * l + 16)
                for tp in range(TB):
                    dve.wait_ge(y_mm, 2 * l + tp + 1)
                    m = v.tensor_tensor(yb[:, tp, :], ps[:, 2 + tp, :], fb_row, ALU.add)
                m.then_inc(yb_done, 1)
                gained(0, 4)
                normalised(1, yb)
                for n in range(14, 17):
                    S(n)
                    second_mod(n)
                S(17)
                gained(1, 2)
                second_mod(17)
                dve.wait_ge(split_done, splits(l, place(2 * KC - 1) + 1, 1))
                add_bias(NEXT, 2 * KC)
                scales(1, S_NORM2)

                def residual(n, k, y):
                    g = (3 * n + 2) * KC + k
                    v.scalar_tensor_tensor(out=xT[:, k, :], in0=y, scalar=modT[:, g:g + 1], in1=xT[:, k, :],
                                           op0=ALU.mult, op1=ALU.add).then_inc(x_done, 1)

                for j in range(GC):
                    S(18 + j)
                    dve.wait_ge(tile_mm, products(l, T_O + GC + j))
                    for i in range(2):
                        residual(0, 2 * j + i, half_bank(O_BANKS[j], i))
                    second_mod(18 + j)
                norm(l, 1)
                for n in range(T_Q + AHEAD, T_IN + AHEAD):
                    S(n)
                    if n < NEXT:
                        second_mod(n)
                dve.wait_ge(split_done, splits(l, place(NEXT - 1) + 1, 1))
                add_bias(NEXT + 2 * KC, KC)

                done = [AHEAD]

                def split_next():
                    S(T_IN + done[0])
                    done[0] += 1

                dve.wait_ge(s_mm, 2 * l + 2)
                v.tensor_copy(scores[:, 1], ps[:, 0:4, :].rearrange("p c (r n) -> p (c r) n", r=4)).then_inc(s_done, 1)
                dve.wait_ge(s_done, 2 * l + 2)
                dve.sem_inc(dve_held, 1)
                v.tensor_copy(ident_2, ident)
                def next_mod(i, m):
                    at_ = i * 3 * SLOTS + T_LAST + NEXT + 3 * m + 2
                    slot = (3 * m + 2) % SLOTS
                    if m % SLOTS == 0:
                        dve.wait_ge(mod_step, MOD_ROUNDS * l + MOD_ROUNDS + m // SLOTS + i)
                    mod_tile(full(l, at_, slot), slot, mod_part[:, m % SLOTS:m % SLOTS + 1])
                    if m == SLOTS - 1:
                        dve.wait_ge(split_done, splits(l, at_, 1))
                        keep_mods(i)

                rest = left.rearrange("p (r n) -> p r n", r=ROWS)
                crow = cand.rearrange("p (h n) -> p h n", h=HEADS)
                crest = left.rearrange("p (h n) -> p h n", h=HEADS)
                picku = pick_u.rearrange("p (h k) -> p h k", h=HEADS)
                hk = [P, HEADS, TOPK]

                def top16(rows):
                    marks = [mark(v.max(val[:, 0:8], src)) for src, _, val, _ in rows]
                    for k, (src, rest_, val, idx) in zip(marks, rows):
                        wait_mark(k)
                        v.max_index(idx[:, 0:8], val[:, 0:8], src)
                        last = mark(v.match_replace(rest_, val[:, 0:8], src, NEG))
                    split_next()
                    wait_mark(last)
                    marks = [mark(v.max(val[:, 8:16], rest_)) for _, rest_, val, _ in rows]
                    for k, (_, rest_, val, idx) in zip(marks, rows):
                        wait_mark(k)
                        m = v.max_index(idx[:, 8:16], val[:, 8:16], rest_)
                    split_next()
                    return m

                def halves(b):
                    for r in range(0, ROWS, 2):
                        m = top16([(scores[:, b, q, :], rest[:, q, :], top_v[:, b, q, :], top_iu[:, b, q, :])
                                   for q in (r, r + 1)])
                    step(m)
                    m = v.tensor_copy(top_i[:, b].rearrange("p h s k -> p (h s k)"),
                                      top_iu[:, b].rearrange("p r k -> p (r k)"))
                    if b == 0:
                        m.then_inc(cand_in, 1)
                    else:
                        step(m)

                def heads(b):
                    dve.wait_ge(cand_done, 2 * l + b + 1)
                    dve.sem_inc(dve_held, 1)
                    for h in range(0, HEADS, 2):
                        m = top16([(crow[:, q, :], crest[:, q, :], pick_v[:, q, :], picku[:, q, :]) for q in (h, h + 1)])
                    step(m)
                    if b == 0:
                        dve.sem_inc(cand_in, 1)
                    v.tensor_scalar(half_u[:, 0, :], pick_u, 4, None, ALU.logical_shift_right)
                    step(v.tensor_scalar(half_u[:, 1, :], pick_u, TOPK - 1, None, ALU.bitwise_and))
                    step(v.tensor_copy(half_f, half_u))
                    for i, buf in enumerate((eq, left)):
                        v.tensor_tensor(buf.rearrange("p (m j) -> p m j", j=TOPK),
                                        half_f[:, i, :].unsqueeze(2).to_broadcast([P, P, TOPK]),
                                        iota[:, 0:TOPK].unsqueeze(1).to_broadcast([P, P, TOPK]), ALU.is_equal)\
                            .then_inc(eq_in, 1)
                        split_next()
                    v.tensor_tensor(picks[:, b, 2, :].rearrange("p (h k) -> p h k", h=HEADS), pick_v,
                                    pick_v[:, :, 0:1].to_broadcast(hk), ALU.subtract).then_inc(exp_in, 1)
                    for i, buf in enumerate((eq, left)):
                        split_next()
                        dve.wait_ge(eq_done, 4 * l + 2 * b + i + 1)
                        m = v.tensor_reduce(picks[:, b, i, :], buf.rearrange("p (m j) -> p m j", j=TOPK), AX.X, ALU.add)
                    step(m, hold=True)

                halves(0)
                halves(1)
                heads(0)
                heads(1)
                while done[0] < (HALF_ROUNDS - GATE_ROUNDS) * SLOTS + AHEAD:
                    split_next()
                for b in range(TB):
                    gate = picks[:, b, 2, :].rearrange("p (h k) -> p h k", h=HEADS)
                    dve.wait_ge(exp_done, 2 * l + b + 1)
                    step(v.tensor_reduce(gsum[:, 0, :], gate, AX.X, ALU.add))
                    step(v.reciprocal(gsum[:, 1, :], gsum[:, 0, :]))
                    v.tensor_tensor(gate, gate, gsum[:, 1, :].unsqueeze(2).to_broadcast(hk), ALU.mult)\
                        .then_inc(picks_done, 1)
                while done[0] < (HALF_ROUNDS - 1) * SLOTS + AHEAD:
                    split_next()
                for b in range(TB):
                    dve.wait_ge(kt_mm, 2 * l + b + 1)
                    col = slice(b * P, (b + 1) * P)
                    v.tensor_copy(kT[:, 0:3:2, col], ps[:, 6 + b, 0:3 * P].rearrange("p (i t) -> p i t", i=3)[:, 0:3:2, :])
                    v.tensor_scalar(kT[:, 1, col], ps[:, 6 + b, P:2 * P], -1.0, None, ALU.mult).then_inc(kt_done, 1)
                while done[0] < HALF_CHUNKS + AHEAD:
                    split_next()

                acts = big.rearrange("p (n t) -> p n t", t=T)

                def hot(n, s):
                    dve.wait_ge(hot_free, l * HOTS + n + 1)
                    for t in range(OT):
                        col = bass.ds(n * OT + t, 1)
                        m = v.tensor_scalar(hot1[:, (s % 2) * OT + t, :], iota[:], kT[:, 0, col], kT[:, 2, col],
                                            ALU.is_equal, ALU.mult)
                    m.then_inc(hot1_ready, 1)

                def gated(g, slot):
                    dve.wait_ge(hot_free, 2 + l * HOTS + 2 * g + 2)
                    rows = ps[:, 4 + 2 * slot:6 + 2 * slot, :].rearrange("p c (t n) -> p (c t) n", t=OT)
                    a = acts[:, 0:HALF_CHUNKS, bass.ds(g * GT, GT)]
                    v.tensor_tensor(a, a, rows[:, :, 0:HD].rearrange("p t n -> p n t"), ALU.mult)
                    dve.wait_ge(stage_free, l * GROUPS + g + 1)
                    v.tensor_copy(stage[:, slot, :].rearrange("p (t n) -> p t n", t=GT), rows[:, :, HD:]).then_inc(g_free, 1)

                def gated_late(g, slot):
                    dve.wait_ge(g_loaded[slot], l * 8 * GROUPS + 8 * g - 8 * slot + 16)
                    a = acts[:, HALF_CHUNKS:CHUNKS, bass.ds(g * GT, GT)]
                    v.tensor_tensor(a, a, stage[:, slot, :].rearrange("p (t n) -> p n t", t=GT), ALU.mult)\
                        .then_inc(g_late_used, 1)

                def split_w(c, s):
                    dve.wait_ge(whi_ready, l * CHUNKS + c + 1)
                    v.tensor_tensor(w_lo[:, s % AHEAD, :], big[:, bass.ds(c * T, T)], w_hi[:, s % AHEAD, :].bitcast(F32),
                                    ALU.subtract).then_inc(wlo_ready, 1)

                def gate_round(i, s, first, last):
                    if not (last and s == SLOTS - 1):
                        hot(i * SLOTS + s + 1, (s + 1) % SLOTS)
                    if s == 1 and not first:
                        gated(2 * i - 1, 1)
                    if s == SLOTS - 1:
                        gated(2 * i, 0)

                dve.wait_ge(kt_done, 2 * l + 2)
                hot(0, 0)
                dve.wait_ge(p_free, PBANKS + l * CHUNKS + HALF_CHUNKS)
                dve.sem_inc(dve_held, 1)

                def in_round(i, first=False, last=False):
                    for s in range(SLOTS):
                        gate_round(i, s, first, last)
                        split(i * SLOTS + T_IN + HALF_CHUNKS + s + AHEAD, (s + AHEAD) % SLOTS, s)

                in_round(0, first=True)
                with dve.Fori(1, HALF_ROUNDS - 1) as i:
                    in_round(i)
                in_round(HALF_ROUNDS - 1, last=True)
                gated(GROUPS - 1, 1)

                for s in range(AHEAD):
                    split_w(s, s)
                dve.wait_ge(p_free, PBANKS + (l + 1) * CHUNKS)
                dve.sem_inc(dve_held, 1)

                def out_round(i, last=False):
                    for s in range(SLOTS):
                        c = i * SLOTS + s
                        if s >= 2:
                            gated_late(2 * i + s - 2, s - 2)
                        split(c + T_OUT + AHEAD, (s + AHEAD) % SLOTS, s)
                        if not (last and s >= SLOTS - AHEAD):
                            split_w(c + AHEAD, (s + AHEAD) % SLOTS)

                with dve.Fori(0, HALF_ROUNDS - 1) as i:
                    out_round(i)
                out_round(HALF_ROUNDS - 1, last=True)
                for s in range(AHEAD):
                    split_w(HALF_CHUNKS + s, s)
                next_mod(0, 0)
                dve.sem_inc(dve_held, 1)

                def mod_round(i, last=False):
                    for s in range(2 * SLOTS):
                        c = i * 2 * SLOTS + HALF_CHUNKS + s
                        j = s + AHEAD
                        split(c + T_OUT + AHEAD, (j + j // 2) % SLOTS, s)
                        split_w(c + AHEAD, s)
                        if j % 2 and not (last and j > 2 * SLOTS):
                            next_mod(i, j // 2)

                with dve.Fori(0, MOD_ROUNDS - 1) as i:
                    mod_round(i)
                mod_round(MOD_ROUNDS - 1, last=True)
                dve.wait_ge(mod_step, MOD_ROUNDS * l + 2 * MOD_ROUNDS)
                dve.sem_inc(dve_held, 1)
                with dve.Fori(2 * MOD_ROUNDS, HALF_ROUNDS - 1) as i:
                    for s in range(SLOTS):
                        c = i * SLOTS + HALF_CHUNKS + s
                        split(c + T_OUT + AHEAD, (s + AHEAD) % SLOTS, s)
                        split_w(c + AHEAD, s)
                for s in range(SLOTS - AHEAD):
                    c = CHUNKS - SLOTS + s
                    S(T_OUT + c + AHEAD)
                    split_w(c + AHEAD, s)
                dve.wait_ge(tile_mm, products(l, TILES - 1))
                for k in range(KC):
                    residual(1, k, half_bank(k // 2, k % 2))
                assert k_step[0] == DVE_STEPS, k_step[0]
            v.memset(ones, 1.0).then_inc(ones_done, 1)
            dve.wait_ge(fin_root, 1)
            v.reciprocal(rstd, rstd).then_inc(dve_norm, 1)
            dve.wait_ge(dve_norm, 2 * LAYERS + 1)
            for k in range(KC):
                m = v.scalar_tensor_tensor(out=hA[:, k, :], in0=xT[:, k, :], scalar=final_g[:, k:k + 1], in1=rstd,
                                           op0=ALU.mult, op1=ALU.mult)
            m.then_inc(fin_done, 1)


def columns(a):
    a = a.reshape(*a.shape[:-1], -1, P)
    return np.swapaxes(a, -1, -2)


def transforms():
    out = np.zeros((P, N_FOURIER), np.float32)
    d = np.arange(HD)
    angle = 2 * np.pi * (np.outer(d, d) % HD) / HD
    pair = np.eye(2)
    out[:, C_COSD:C_COSD + P] = np.kron(pair, np.cos(angle)) / np.sqrt(HD)
    out[:, C_SIND:C_SIND + P] = -np.kron(pair, np.sin(angle)) / np.sqrt(HD)
    s = np.arange(T)
    angle = 2 * np.pi * (np.outer(s, s) % T) / T
    m = np.stack([np.cos(angle), np.sin(angle)]) / np.sqrt(T)
    out[:, C_ID:C_ID + P] = np.eye(P)
    out[:, C_DFT:] = m.reshape(2, TB, P, T).transpose(2, 0, 1, 3).reshape(P, 2 * TB * T)
    return out


def by_columns(w):
    l = w.shape[0]
    return w.reshape(l, KC, P, -1, P).transpose(0, 3, 2, 1, 4).reshape(l, -1, P, D)


def kernel(**inputs):
    import concourse.bacc as bacc
    from concourse.bass_utils import run_bass_kernel_spmd

    a = {k: np.asarray(v) for k, v in inputs.items()}
    L = LAYERS
    arrays = {}
    arrays["x_in"] = columns(a["x"][0]).transpose(1, 2, 0)
    arrays["c_in"] = a["c"]
    arrays["iota_in"] = np.tile(np.arange(P, dtype=np.float32), (P, 1))
    arrays["fourier_in"] = transforms()
    arrays["small_in"] = np.concatenate([
        columns(a["norm1_g"]), columns(a["norm2_g"]),
        columns(np.concatenate([a["gain_a"], a["gain_b"]], -1)),
        a["gmlp_bs"].transpose(0, 2, 1),
        columns(a["mod_b"]),
        a["fnet_w"].reshape(L, GC, P, HD).transpose(0, 2, 1, 3).reshape(L, P, GC * HD),
        a["gmlp_ws"].transpose(0, 3, 1, 2).reshape(L, P, HEADS * P)], -1)
    arrays["fb_in"] = a["fnet_b"].reshape(L, WIDTH)
    keys = np.stack([a["peer_k1"], a["peer_k2"]], 2)
    arrays["keys_in"] = keys.transpose(0, 4, 1, 2, 3).reshape(L, P, ROWS, KEYS)
    w = a["w_in"]
    v_and_u = [w[..., i:i + WIDTH].reshape(L, GC, 2, P, WIDTH).transpose(0, 1, 3, 2, 4).reshape(L, GC, P, D)
               for i in (WIDTH, 0)]
    arrays["w_in_in"] = np.concatenate([v_and_u[0], by_columns(w[..., 2 * WIDTH:]), v_and_u[1]], 1)
    w = a["w_out"].reshape(L, 2, GC, P, GC, 2, P)
    arrays["w_out_in"] = w.transpose(0, 1, 4, 3, 5, 2, 6).reshape(L, KC, P, D)
    arrays["wq_in"] = by_columns(a["peer_wq"])
    arrays["mod_in"] = a["mod_w"].transpose(0, 2, 1).reshape(L, MODS, P, D)
    u = a["peer_u"].reshape(L, KEYS, CHUNKS, KC, P).transpose(0, 2, 4, 3, 1)
    arrays["u_in"] = u.reshape(L, CHUNKS, P, D)
    arrays["v_in"] = a["peer_v"].reshape(L, KEYS, CHUNKS, D).transpose(0, 2, 1, 3)
    arrays["final_in"] = columns(a["final_g"])
    arrays = {k: np.ascontiguousarray(v) for k, v in arrays.items()}

    nc = bacc.Bacc("TRN2", target_bir_lowering=False, num_devices=1)
    aps = {k: nc.dram_tensor(k, v.shape, F32, kind="ExternalInput").ap() for k, v in arrays.items()}
    g_late = nc.dram_tensor("g_late", (GROUPS, P, GT * HD), F32, kind="Internal").ap()
    out = nc.dram_tensor("out", (P, KC, T), F32, kind="ExternalOutput").ap()
    build(nc, **aps, g_late=g_late, out=out)
    r = run_bass_kernel_spmd(nc, [arrays], core_ids=[0])
    y = r.results[0]["out"]
    return np.ascontiguousarray(y.transpose(2, 1, 0).reshape(1, T, D))
```
